# Optimizing a Trainium2 kernel written in Bass

```python
import math
import jax, jax.numpy as jnp
from jax import lax
import numpy as np

D_MODEL = 2048
BATCH = 1
SEQ = 512
DEPTH = 2
DEC_BATCH = 8
DEC_SEQ = 1
PAST_LEN = 4096
PAGE_SIZE = 128

HEAD_DIM = 128
H_HG = 4
H_ML = 6
H_RT = 6
W_HG = H_HG * HEAD_DIM
W_ML = H_ML * HEAD_DIM
W_RT = H_RT * HEAD_DIM
D_MIX = W_HG + W_ML + W_RT
CONV_W = 4
HG_CHUNK = 16
CHUNK = 64
ROPE_BASE = 10000.0
EPS = 1e-6
COL_SIZES = (W_HG, W_HG, W_HG,
             W_ML, W_ML, W_ML, H_ML, H_ML,
             W_RT, W_RT, W_RT,
             D_MIX)
N_IN = sum(COL_SIZES)

kernel_name = 'hymba_hgrn2_mlstm_retnet_step'

def _rmsnorm(x, g):
    xf = x.astype(jnp.float32)
    y = xf * lax.rsqrt(jnp.mean(xf * xf, axis=-1, keepdims=True) + EPS)
    return (y * g.astype(jnp.float32)).astype(x.dtype)

def _to_heads(x, n_heads):
    b, t, _ = x.shape
    return x.reshape(b, t, n_heads, -1).transpose(0, 2, 1, 3).astype(jnp.float32)

def _to_chunks(x, chunk):
    b, h, t = x.shape[:3]
    x = x.reshape((b, h, t // chunk, chunk) + x.shape[3:])
    return jnp.moveaxis(x, 2, 0)

def _from_chunks(x):
    n, b, h, c = x.shape[:4]
    return jnp.moveaxis(x, 0, 2).reshape((b, h, n * c) + x.shape[4:])

def _head_norm(o, gain, center):
    if center:
        o = o - jnp.mean(o, axis=-1, keepdims=True)
    o = o * lax.rsqrt(jnp.mean(o * o, axis=-1, keepdims=True) + EPS)
    b, h, t, d = o.shape
    return o.transpose(0, 2, 1, 3).reshape(b, t, h * d) * gain.astype(jnp.float32)

def _rope(x, pos):
    half = x.shape[-1] // 2
    inv_freq = ROPE_BASE ** (-jnp.arange(half, dtype=jnp.float32) / half)
    ang = pos[:, None] * inv_freq[None, :]
    cos, sin = jnp.cos(ang), jnp.sin(ang)
    x1, x2 = x[..., :half], x[..., half:]
    return jnp.concatenate([x1 * cos - x2 * sin, x1 * sin + x2 * cos], axis=-1)

def _hgrn2_chunked(q, k, v, log_f, s0):
    t = q.shape[2]
    chunk = math.gcd(t, HG_CHUNK)
    mask = jnp.tril(jnp.ones((chunk, chunk), dtype=bool))

    def body(s, inp):
        qc, kc, vc, gc = inp
        b = jnp.cumsum(gc, axis=2)
        inter = jnp.einsum('bhtk,bhkv->bhtv', qc * jnp.exp(b), s)
        diff = b[:, :, :, None, :] - b[:, :, None, :, :]
        decay = jnp.exp(jnp.where(mask[:, :, None], diff, -jnp.inf))
        a = jnp.einsum('bhtk,bhsk,bhtsk->bhts', qc, kc, decay)
        intra = jnp.einsum('bhts,bhsv->bhtv', a, vc)
        b_last = b[:, :, -1:, :]
        s_new = (jnp.exp(b_last[:, :, 0, :])[..., None] * s
                 + jnp.einsum('bhsk,bhsv->bhkv', kc * jnp.exp(b_last - b), vc))
        return s_new, inter + intra

    s_fin, o = lax.scan(body, s0.astype(jnp.float32),
                        (_to_chunks(q, chunk), _to_chunks(k, chunk),
                         _to_chunks(v, chunk), _to_chunks(log_f, chunk)))
    return _from_chunks(o), s_fin

def _mlstm_chunked(q, k, v, ig, lf, c0, n0, m0):
    t = q.shape[2]
    chunk = math.gcd(t, CHUNK)
    mask = jnp.tril(jnp.ones((chunk, chunk), dtype=bool))

    def body(carry, inp):
        c, n, m = carry
        qc, kc, vc, ic, fc = inp
        b = jnp.cumsum(fc, axis=-1)
        d = jnp.where(mask, b[..., :, None] - b[..., None, :] + ic[..., None, :], -jnp.inf)
        m_inter = b + m[..., None]
        m_t = jnp.maximum(m_inter, jnp.max(d, axis=-1))
        inter_w = jnp.exp(m_inter - m_t)
        sc = jnp.einsum('bhtk,bhsk->bhts', qc, kc) * jnp.exp(d - m_t[..., None])
        num = (inter_w[..., None] * jnp.einsum('bhvk,bhtk->bhtv', c, qc)
               + jnp.einsum('bhts,bhsv->bhtv', sc, vc))
        den = inter_w * jnp.einsum('bhk,bhtk->bht', n, qc) + jnp.sum(sc, axis=-1)
        h = num / jnp.maximum(jnp.abs(den), jnp.exp(-m_t))[..., None]
        b_last = b[..., -1]
        w_s = b_last[..., None] - b + ic
        m_new = jnp.maximum(b_last + m, jnp.max(w_s, axis=-1))
        decay_c = jnp.exp(b_last + m - m_new)
        w_s = jnp.exp(w_s - m_new[..., None])
        c_new = decay_c[..., None, None] * c + jnp.einsum('bhs,bhsv,bhsk->bhvk', w_s, vc, kc)
        n_new = decay_c[..., None] * n + jnp.einsum('bhs,bhsk->bhk', w_s, kc)
        return (c_new, n_new, m_new), h

    (c_f, n_f, m_f), o = lax.scan(
        body, (c0.astype(jnp.float32), n0.astype(jnp.float32), m0.astype(jnp.float32)),
        (_to_chunks(q, chunk), _to_chunks(k, chunk), _to_chunks(v, chunk),
         _to_chunks(ig, chunk), _to_chunks(lf, chunk)))
    return _from_chunks(o), c_f, n_f, m_f

def _retention_chunked(q, k, v, s0):
    t, n_heads = q.shape[2], q.shape[1]
    chunk = math.gcd(t, CHUNK)
    mask = jnp.tril(jnp.ones((chunk, chunk), dtype=bool))
    log_g = jnp.log1p(-(2.0 ** (-5.0 - jnp.arange(n_heads, dtype=jnp.float32))))
    j = jnp.arange(chunk, dtype=jnp.float32)
    inter_d = jnp.exp(log_g[:, None] * (j + 1.0))
    rel = jnp.where(mask, j[:, None] - j[None, :], 0.0)
    intra_d = jnp.where(mask, jnp.exp(log_g[:, None, None] * rel), 0.0)
    state_d = jnp.exp(log_g[:, None] * (chunk - 1.0 - j))
    chunk_d = jnp.exp(log_g * chunk)

    def body(s, inp):
        qc, kc, vc = inp
        inter = inter_d[None, :, :, None] * jnp.einsum('bhtk,bhkv->bhtv', qc, s)
        sc = jnp.einsum('bhtk,bhsk->bhts', qc, kc) * intra_d[None]
        intra = jnp.einsum('bhts,bhsv->bhtv', sc, vc)
        s_new = (chunk_d[None, :, None, None] * s
                 + jnp.einsum('bhsk,bhsv->bhkv', kc * state_d[None, :, :, None], vc))
        return s_new, inter + intra

    s_fin, o = lax.scan(body, s0.astype(jnp.float32),
                        (_to_chunks(q, chunk), _to_chunks(k, chunk), _to_chunks(v, chunk)))
    return _from_chunks(o), s_fin

def _layer(x, c, pos, state, lb, g_norm, w_ada, b_ada, w_in, conv_w, conv_b,
           b_i, b_f, skip, w_gn, w_out):
    hg_s, ml_c, ml_n, ml_m, ml_conv, rt_s = state
    t = x.shape[1]
    mod = jax.nn.silu(c) @ w_ada + b_ada
    shift, scale, gate = jnp.split(mod, 3, axis=-1)
    h = _rmsnorm(x, g_norm) * (1.0 + scale[:, None, :]) + shift[:, None, :]
    cols = jnp.split(h @ w_in, np.cumsum(COL_SIZES)[:-1].tolist(), axis=-1)
    hq, hf, hi, mq, mk, mv, mi, mf, rq, rk, rv, z = cols

    lb_h = lb.reshape(H_HG, 1, HEAD_DIM).astype(jnp.float32)
    a = _to_heads(hf, H_HG)
    log_f = jnp.logaddexp(jnp.log(lb_h), jnp.log1p(-lb_h) + jax.nn.log_sigmoid(a))
    k_hg = (1.0 - lb_h) * jax.nn.sigmoid(-a)
    o_hg, hg_s_new = _hgrn2_chunked(_to_heads(hq, H_HG) * HEAD_DIM ** -0.5, k_hg,
                                    _to_heads(hi, H_HG), log_f, hg_s)

    qk_raw = jnp.concatenate([mq, mk], axis=-1)
    xpad = jnp.concatenate([ml_conv.astype(qk_raw.dtype), qk_raw], axis=1)
    conv = conv_b + sum(xpad[:, j:j + t, :] * conv_w[j] for j in range(CONV_W))
    new_conv = xpad[:, t:, :]
    q_c, k_c = jnp.split(jax.nn.silu(conv), 2, axis=-1)
    ig = (mi + b_i).astype(jnp.float32).transpose(0, 2, 1)
    lf = jax.nn.log_sigmoid((mf + b_f).astype(jnp.float32)).transpose(0, 2, 1)
    o_ml, ml_c_new, ml_n_new, ml_m_new = _mlstm_chunked(
        _to_heads(q_c, H_ML), _to_heads(k_c, H_ML) * HEAD_DIM ** -0.5, _to_heads(mv, H_ML),
        ig, lf, ml_c, ml_n, ml_m)

    q_r = _rope(_to_heads(rq, H_RT), pos)
    k_r = _rope(_to_heads(rk, H_RT), pos) * HEAD_DIM ** -0.5
    o_rt, rt_s_new = _retention_chunked(q_r, k_r, _to_heads(rv, H_RT), rt_s)

    o = jnp.concatenate([
        _head_norm(o_hg, w_gn[:W_HG], False),
        _head_norm(o_ml, w_gn[W_HG:W_HG + W_ML], True) + skip * q_c.astype(jnp.float32),
        _head_norm(o_rt, w_gn[W_HG + W_ML:], True)], axis=-1)
    o = o.astype(x.dtype) * jax.nn.silu(z)
    y = x + gate[:, None, :] * (o @ w_out)
    return y, (hg_s_new, ml_c_new, ml_n_new, ml_m_new, new_conv, rt_s_new)

def setup_inputs(seed: int = 0) -> dict:
    key = jax.random.key(seed)
    ks = jax.random.split(key, 24)

    def nrm(k, shape, s):
        return s * jax.random.normal(k, shape, dtype=jnp.float32)

    return {
        'x_prompt': nrm(ks[0], (BATCH, SEQ, D_MODEL), 1.0),
        'x_sample': nrm(ks[1], (DEC_BATCH, DEC_SEQ, D_MODEL), 1.0),
        'state_hgrn': nrm(ks[2], (DEPTH, DEC_BATCH, H_HG, HEAD_DIM, HEAD_DIM), 0.5),
        'state_mlstm_C': nrm(ks[3], (DEPTH, DEC_BATCH, H_ML, HEAD_DIM, HEAD_DIM), 0.5),
        'state_mlstm_n': nrm(ks[4], (DEPTH, DEC_BATCH, H_ML, HEAD_DIM), 0.5),
        'state_mlstm_m': nrm(ks[5], (DEPTH, DEC_BATCH, H_ML), 1.0),
        'state_mlstm_conv': nrm(ks[6], (DEPTH, DEC_BATCH, CONV_W - 1, 2 * W_ML), 1.0),
        'state_ret': nrm(ks[7], (DEPTH, DEC_BATCH, H_RT, HEAD_DIM, HEAD_DIM), 0.5),
        'c_prompt': nrm(ks[8], (BATCH, D_MODEL), 1.0),
        'c_sample': nrm(ks[9], (DEC_BATCH, D_MODEL), 1.0),
        'g_norm': 1.0 + nrm(ks[10], (DEPTH, D_MODEL), 0.02),
        'w_ada': nrm(ks[11], (DEPTH, D_MODEL, 3 * D_MODEL), 0.5 * D_MODEL ** -0.5),
        'b_ada': nrm(ks[12], (DEPTH, 3 * D_MODEL), 0.02),
        'w_in': nrm(ks[13], (DEPTH, D_MODEL, N_IN), D_MODEL ** -0.5),
        'hgrn_lb': nrm(ks[14], (DEPTH, W_HG), 1.0),
        'mlstm_conv_w': nrm(ks[15], (DEPTH, CONV_W, 2 * W_ML), CONV_W ** -0.5),
        'mlstm_conv_b': nrm(ks[16], (DEPTH, 2 * W_ML), 0.02),
        'mlstm_b_i': nrm(ks[17], (DEPTH, H_ML), 0.1),
        'mlstm_b_f': jnp.linspace(3.0, 6.0, H_ML, dtype=jnp.float32)[None, :] + nrm(ks[18], (DEPTH, H_ML), 0.1),
        'mlstm_skip': 1.0 + nrm(ks[19], (DEPTH, W_ML), 0.02),
        'w_gn': 1.0 + nrm(ks[20], (DEPTH, D_MIX), 0.02),
        'w_out': nrm(ks[21], (DEPTH, D_MIX, D_MODEL), D_MIX ** -0.5),
        'g_final': 1.0 + nrm(ks[22], (D_MODEL,), 0.02),
    }

def reference(x_prompt, x_sample, state_hgrn, state_mlstm_C, state_mlstm_n, state_mlstm_m,
              state_mlstm_conv, state_ret, c_prompt, c_sample, g_norm, w_ada, b_ada, w_in,
              hgrn_lb, mlstm_conv_w, mlstm_conv_b, mlstm_b_i, mlstm_b_f, mlstm_skip, w_gn,
              w_out, g_final):
    f32 = jnp.float32
    lb_cum = jnp.cumsum(jax.nn.softmax(hgrn_lb.astype(f32), axis=0), axis=0)
    lb_all = lb_cum - lb_cum[0:1]
    b_p, t_p = x_prompt.shape[0], x_prompt.shape[1]
    t_s = x_sample.shape[1]
    pos_p = jnp.arange(t_p, dtype=f32)
    pos_s = PAST_LEN + jnp.arange(t_s, dtype=f32)
    init_p = (jnp.zeros((b_p, H_HG, HEAD_DIM, HEAD_DIM), f32),
              jnp.zeros((b_p, H_ML, HEAD_DIM, HEAD_DIM), f32),
              jnp.zeros((b_p, H_ML, HEAD_DIM), f32),
              jnp.zeros((b_p, H_ML), f32),
              jnp.zeros((b_p, CONV_W - 1, 2 * W_ML), x_prompt.dtype),
              jnp.zeros((b_p, H_RT, HEAD_DIM, HEAD_DIM), f32))
    yp, ys = x_prompt, x_sample
    new_p, new_s = [], []
    for l in range(DEPTH):
        lw = (g_norm[l], w_ada[l], b_ada[l], w_in[l], mlstm_conv_w[l], mlstm_conv_b[l],
              mlstm_b_i[l], mlstm_b_f[l], mlstm_skip[l], w_gn[l], w_out[l])
        yp, sp = _layer(yp, c_prompt, pos_p, init_p, lb_all[l], *lw)
        st_l = (state_hgrn[l], state_mlstm_C[l], state_mlstm_n[l], state_mlstm_m[l],
                state_mlstm_conv[l], state_ret[l])
        ys, ss = _layer(ys, c_sample, pos_s, st_l, lb_all[l], *lw)
        new_p.append(sp)
        new_s.append(ss)
    y_prompt = _rmsnorm(yp, g_final)
    y_sample = _rmsnorm(ys, g_final)
    hgrn_p = jnp.stack([s[0] for s in new_p])
    mlstm_C_p = jnp.stack([s[1] for s in new_p])
    mlstm_n_p = jnp.stack([s[2] for s in new_p])
    mlstm_m_p = jnp.stack([s[3] for s in new_p])
    mlstm_conv_p = jnp.stack([s[4] for s in new_p])
    ret_p = jnp.stack([s[5] for s in new_p])
    hgrn_s = jnp.stack([s[0] for s in new_s])
    mlstm_C_s = jnp.stack([s[1] for s in new_s])
    mlstm_n_s = jnp.stack([s[2] for s in new_s])
    mlstm_m_s = jnp.stack([s[3] for s in new_s])
    mlstm_conv_s = jnp.stack([s[4] for s in new_s])
    ret_s = jnp.stack([s[5] for s in new_s])
    return (y_prompt, y_sample, hgrn_p, mlstm_C_p, mlstm_n_p, mlstm_m_p, mlstm_conv_p, ret_p,
            hgrn_s, mlstm_C_s, mlstm_n_s, mlstm_m_s, mlstm_conv_s, ret_s)


_drawn_inputs = setup_inputs


def setup_inputs(seed=0):
    import zlib

    import numpy as np

    out = dict(_drawn_inputs(seed))
    spreads = {}
    factors = {'mlstm_skip': 8.0, 'w_gn': 8.0, 'g_final': 2.826}
    for name, (base, spread) in spreads.items():
        noise = np.random.default_rng([zlib.crc32(name.encode()), seed]).standard_normal(out[name].shape)
        drawn = base * np.exp(spread * noise) if base else spread * noise
        out[name] = __import__('jax').numpy.asarray(drawn.astype(out[name].dtype))
    for name, factor in factors.items():
        out[name] = (out[name] * factor).astype(out[name].dtype)
    return out
```

```python
from contextlib import ExitStack

import numpy as np
import concourse.bass as bass
from concourse import mybir

F32 = mybir.dt.float32
U32 = mybir.dt.uint32
ALU = mybir.AluOpType
ACT = mybir.ActivationFunctionType

P = 128
DEPTH, D, T, NS, HD = 2, 2048, 512, 8, 128
KB = D // P
TOK = T + NS
HALF = TOK // 2
CH = 128
NC = T // CH
H_HG, H_ML, H_RT = 4, 6, 6
NH = H_HG + H_ML + H_RT
W_HG, W_ML, W_RT = H_HG * HD, H_ML * HD, H_RT * HD
COL_HG = (W_HG, 0, 2 * W_HG)
COL_ML = (3 * W_HG, 3 * W_HG + W_ML, 3 * W_HG + 2 * W_ML)
COL_GATES = 3 * W_HG + 3 * W_ML
COL_RT = tuple(COL_GATES + 2 * H_ML + j * W_RT for j in range(3))
COL_Z = COL_GATES + 2 * H_ML + 3 * W_RT
CONV_W = 4
PAD = CONV_W - 1
EPS = 1e-6
SCALE = HD ** -0.5
PAST = 4096
LEVELS = 7
SLOTS = 4
ADA_N = 512
ADA_GROUPS = 3 * D // ADA_N
USES = ADA_GROUPS + NH + KB // SLOTS

R_GN, R_SKIP, R_CW = 0, NH, NH + H_ML
R_CB = R_CW + CONV_W * 2 * H_ML
R_NORM = R_CB + 2 * H_ML
R_LB = R_NORM + KB
N_PRM = R_LB + DEPTH * H_HG
N_BIAS = 3 * KB + KB

C_ID, C_ROT, C_NEG, C_LEV = 0, 128, 256, 384
C_RST = C_LEV + LEVELS * 128
C_SUM = C_RST + T
C_ONE = C_SUM + 9
N_CST = C_ONE + 128
HC_D, HC_IN, HC_ST, HC_CD, HC_G = 0, 128, 640, 641, 645
N_HC = 653


STORES = {"hg": 2, "ml": 8, "rt": 2}
STORES_PER_LAYER = 3 + sum(n * STORES[t] for n, t in ((H_HG, "hg"), (H_ML, "ml"), (H_RT, "rt")))


def constants():
    f = np.float32
    i = np.arange(128)
    c = np.zeros((128, N_CST), f)
    c[:, C_ID:C_ID + 128] = np.eye(128)
    for m in range(64):
        c[m + 64, C_ROT + m] = -1.0
        c[m, C_ROT + m + 64] = 1.0
    c[:, C_NEG:C_NEG + 128] = np.where(i[None, :] >= i[:, None], 0.0, -1e30)
    for v in range(LEVELS):
        h = 64 >> v
        same = i[:, None] // (2 * h) == i[None, :] // (2 * h)
        c[:, C_LEV + 128 * v:C_LEV + 128 * v + 128] = same & (i[:, None] // h % 2 == 0) & (i[None, :] // h % 2 == 1)
    inv = (f(10000.0) ** (-np.arange(64, dtype=f) / f(64))).astype(f)
    pos = np.concatenate([np.arange(T, dtype=f), np.full(NS, PAST, f)])
    ang = (pos[None, :] * inv[:, None]).astype(f)
    ang = np.concatenate([ang, ang], 0)
    c[:, C_RST:C_RST + T] = np.arange(T) % CH != 0
    for j in range(4):
        for s in range(9):
            c[32 * j + s, C_SUM + s] = 1.0
    c[:, C_ONE:C_ONE + 128] = 1.0
    hc = np.zeros((H_RT, 128, N_HC), f)
    for h in range(H_RT):
        lg = np.log1p(-(2.0 ** (-5.0 - h)))
        hc[h, :, HC_D:HC_D + 128] = np.where(i[None, :] >= i[:, None], np.exp(lg * np.maximum(i[None, :] - i[:, None], 0)), 0)
        hc[h, :, HC_IN:HC_IN + T] = np.exp(lg * (np.arange(T) % CH + 1.0))[None, :]
        hc[h, :, HC_ST] = np.exp(lg * (CH - 1.0 - i))
        hc[h, :, HC_CD:HC_CD + NC] = np.exp(lg * CH)
        hc[h, :, HC_G:HC_G + NS] = np.exp(lg)
    sel = np.zeros((H_ML, H_ML, HD), f)
    for h in range(H_ML):
        sel[h, h] = 1.0
    rp = np.concatenate([np.cos(ang), np.sin(ang)], 1).astype(f)
    return c, hc, rp, sel


def program(nc, x_prompt, x_sample, st_hg, st_c, st_n, st_m, st_conv, st_rt, c_prompt, c_sample, g_norm,
            w_ada, b_ada, w_in, hgrn_lb, conv_w, conv_b, b_i, b_f, skip, w_gn, w_out, g_final,
            cst_d, hc_d, rope_d, sel_d,
            y_p, y_s, hg_p, c_p, n_p, m_p, conv_p, rt_p, hg_s, c_s, n_s, m_s, conv_s, rt_s):
    with ExitStack() as ctx:
        def sb(name, *shape):
            return ctx.enter_context(nc.sbuf_tensor(name, list(shape), F32))

        def sem(name):
            return ctx.enter_context(nc.semaphore(name))

        pj = ctx.enter_context(nc.psum_tensor("pj", [P, 4, 512], F32))
        mx = ctx.enter_context(nc.psum_tensor("mx", [P, 4, 512], F32))
        cst = sb("cst", P, N_CST)
        y = sb("y", P, KB, TOK)
        h = sb("h", P, KB, TOK)
        o = sb("o", P, KB, TOK)
        ring = sb("ring", P, SLOTS, KB * P)
        x0, x1 = sb("x0", P, PAD + TOK), sb("x1", P, PAD + TOK)
        v, z, q, k = (sb(n, P, TOK) for n in ("v", "z", "q", "k"))
        t1, t2, t3, t4 = (sb(n, P, TOK) for n in ("t1", "t2", "t3", "t4"))
        lev = sb("lev", P, LEVELS, T)
        qd, dt = sb("qd", P, T), sb("dt", P, T)
        a = sb("a", P, NC, CH)
        kt = sb("kt", P, NC, HD)
        vt = sb("vt", P, NC, HD + 1)
        st = sb("st", P, NC, HD + 1)
        ss = sb("ss", P, NS, HD)
        ho = sb("ho", P, NC + 1, HD)
        ct = sb("ct", P, HD)
        big = lev[:, 4:6, :].rearrange("p a b -> p (a b)")
        r6 = lev[0:H_ML, LEVELS - 1, :]
        levf = lev[:].rearrange("p a b -> p (a b)")
        hc, rope_t = levf[:, 0:N_HC], levf[:, N_HC:N_HC + 2 * TOK]
        selh = sb("selh", H_ML, HD)
        cvr = sb("cvr", NS * PAD, 2, HD)
        cvc = sb("cvc", P, 2, NS * PAD)
        cvo = sb("cvo", PAD + NS, 2, HD)
        nr = sb("nr", NS, HD)
        sr = sb("sr", NS, 3, HD)
        sw = sb("sw", NS, HD)
        sm = sb("sm", P, 64)
        bst = sb("bst", P, NC + 1, 6)
        bag = sb("bag", P, NC + 1, 2)
        rstd = sb("rstd", P, NC + 1)
        prm = sb("prm", P, N_PRM)
        bia = sb("bia", P, N_BIAS)
        prow = sb("prow", P, P)
        brow = sb("brow", P, P)
        lbc = sb("lbc", P, 3, H_HG)
        sct = sb("sct", P, KB, 32)
        mod = sb("mod", P, 3 * KB, 9)
        ag = sb("ag", P, KB, 9)
        gw = sb("gw", P, KB, 2 * H_ML)
        gb = sb("gb", P, 2)
        iw6 = sb("iw6", H_ML, T)
        gcol = sb("gcol", P, H_ML, 4, NC)
        gs = sb("gs", NS, H_ML, 3)
        gsb = sb("gsb", P, H_ML, NS)
        g8 = sb("g8", H_ML, 12, NS)
        g4 = sb("g4", H_ML, 4, NC)
        m6 = sb("m6", H_ML, NS)

        ident = cst[:, C_ID:C_ID + 128]
        ones = cst[:, C_ONE:C_ONE + 128]
        ssum = cst[:, C_SUM:C_SUM + 9]

        spare = sem("spare")
        const_in, x_in, prm_in, gates_in = sem("const_in"), sem("x_in"), sem("prm_in"), sem("gates_in")
        w_in_s = [sem(f"weights{j}") for j in range(SLOTS)]
        w_used = sem("w_used")
        xt_ready, xt_taken = sem("xt_ready"), sem("xt_taken")
        silu_c, sct_ready, sct_taken = sem("silu_c"), sem("sct_ready"), sem("sct_taken")
        init_done, c_exp, lb_diff, lb_ln = sem("init_done"), sem("c_exp"), sem("lb_diff"), sem("lb_ln")
        prm_tr, prm_taken = sem("prm_tr"), sem("prm_taken")
        ada_taken, ada_sum, mod_ready = sem("ada_taken"), sem("ada_sum"), sem("mod_ready")
        ms_ready, rs_made = sem("ms_ready"), sem("rs_made")
        sq_ready, sq_used, rs_ready = sem("sq_ready"), sem("sq_used"), sem("rs_ready")
        hn_ready, h_ready, hs_ready = sem("hn_ready"), sem("h_ready"), sem("hs_ready")
        taken = sem("taken")
        out_added = sem("out_added")
        head_done = sem("head_done")
        ps = {n: sem("p_" + n) for n in ("rot_q", "rot_k", "score", "tr", "u", "outer", "o", "os", "back", "cback",
                                         "conv", "bcast", "ostr")}
        vs = {n: sem("v_" + n) for n in ("qk", "a", "chain", "ss", "ho", "blk", "rot_q", "lev", "pred", "lf", "b",
                                         "conv_q", "conv_k", "silu", "r", "qd", "osc", "nrow", "kw", "d1", "var")}
        as_ = {n: sem("a_" + n) for n in ("vt", "kt", "sr", "e1", "l1", "e2", "l2", "kk", "eb", "kw", "lev", "cvc",
                                          "cvo", "dt", "silu", "z", "ct", "rs")}
        gsem = {n: sem("g_" + n) for n in ("proj", "a1", "v1", "a2", "tr", "col", "v2")}
        state_in, aux_in, stored = sem("state_in"), sem("aux_in"), sem("stored")
        fin_n, fin_t, fin_e, out_st = sem("fin_n"), sem("fin_t"), sem("fin_e"), sem("out_st")

        xrow = o[:].rearrange("p k t -> p (k t)")[:, 0:4 * D].rearrange("p (b d) -> p b d", b=4)
        hrow = h[:].rearrange("p k t -> p (k t)")
        crow, srow, e_row = hrow[0:9, 0:D], hrow[0:NS, D:2 * D], hrow[0:9, 2 * D:3 * D]
        yrow = xrow
        ysrow = ring[0:NS, 0, 0:D]

        def gi(l, base, i):
            return l * NH + base + i

        def auxc(l, kind, i):
            before = l * 16 * (4 * H_ML + H_RT + 1)
            return i * 64 + (before + 64) if kind == "ml" else i * 16 + (before + 64 * H_ML + 32)

        def scorec(l, kind, i, x):
            before = l * (H_HG * (LEVELS + 1) + H_ML + H_RT)
            if kind == "hg":
                return i * (LEVELS + 1) + (before + x)
            return i + (before + H_HG * (LEVELS + 1) + (H_ML if kind == "rt" else 0) + x)

        def held(e):
            e.sem_inc(spare, 1)

        def ht(g, j):
            return g * 4 + j + 3

        block = ctx.enter_context(nc.Block())
        GROUPS = ((H_HG, 0, "hg", COL_HG), (H_ML, H_HG, "ml", COL_ML), (H_RT, H_HG + H_ML, "rt", COL_RT))

        @block.sync
        def _(e):
            def load(slot, use, src, dst=None):
                e.wait_ge(w_used, (use - 1) * SLOTS + slot + 1)
                held(e)
                e.dma_start(ring[:, slot, :] if dst is None else dst, src).then_inc(w_in_s[slot], 16)

            def first_load(slot, use, src, dst):
                e.dma_start(dst, src).then_inc(w_in_s[slot], 16)

            e.dma_start(cst[:], cst_d).then_inc(const_in, 16)
            e.dma_start(crow[0:1, :], c_prompt).then_inc(x_in, 16)
            e.dma_start(crow[1:9, :], c_sample).then_inc(x_in, 16)
            e.dma_start(srow, x_sample.rearrange("b t d -> (b t) d")).then_inc(x_in, 16)
            e.dma_start(xrow, x_prompt[0].rearrange("(b p) d -> p b d", p=P)).then_inc(x_in, 16)
            for l in range(DEPTH):
                wa = w_ada[l].rearrange("(k p) n -> p k n", p=P)
                wi = w_in[l].rearrange("(k p) n -> p k n", p=P)
                wo = w_out[l].rearrange("(k p) n -> p k n", p=P)
                u0 = l * USES
                for n in range(ADA_GROUPS):
                    for s in range(SLOTS):
                        dst = ring[:, s, :].rearrange("p (k n) -> p k n", k=KB // SLOTS)
                        (first_load if u0 + n == 0 else load)(
                            s, u0 + n, wa[:, 4 * s:4 * s + 4, n * ADA_N:(n + 1) * ADA_N], dst)
                for count, base, kind, cols in GROUPS:
                    with e.Fori(0, count) as i:
                        for s in range(SLOTS):
                            col = i * HD + (cols[s] if s < 3 else COL_Z + base * HD)
                            load(s, i + (u0 + ADA_GROUPS + base), wi[:, :, bass.ds(col, HD)],
                                 ring[:, s, :].rearrange("p (k n) -> p k n", k=KB))
                for n in range(KB):
                    load(n % SLOTS, u0 + ADA_GROUPS + NH + n // SLOTS, wo[:, :, n * P:(n + 1) * P],
                         ring[:, n % SLOTS, :].rearrange("p (k n) -> p k n", k=KB))
            e.wait_ge(fin_e, KB + 4)
            e.dma_start(y_p[0].rearrange("(b p) d -> p b d", p=P), yrow).then_inc(out_st, 16)
            e.dma_start(y_s.rearrange("b t d -> (b t) d"), ysrow).then_inc(out_st, 16)
            e.wait_ge(out_st, 32)

        @block.gpsimd
        def _(e):
            for l in range(DEPTH):
                if l:
                    e.wait_ge(prm_taken, 2 * l)
                    e.wait_ge(gsem["v2"], l)
                    held(e)
                e.dma_start(prow[R_GN:R_GN + NH, :], w_gn[l].rearrange("(r d) -> r d", d=HD)).then_inc(prm_in, 16)
                e.dma_start(prow[R_SKIP:R_SKIP + H_ML, :], skip[l].rearrange("(r d) -> r d", d=HD)).then_inc(prm_in, 16)
                e.dma_start(prow[R_CW:R_CB, :], conv_w[l].rearrange("j (r d) -> (j r) d", d=HD)).then_inc(prm_in, 16)
                e.dma_start(prow[R_CB:R_NORM, :], conv_b[l].rearrange("(r d) -> r d", d=HD)).then_inc(prm_in, 16)
                e.dma_start(prow[R_NORM:R_LB, :], g_norm[l].rearrange("(r d) -> r d", d=HD)).then_inc(prm_in, 16)
                e.dma_start(prow[R_LB:N_PRM, :], hgrn_lb.rearrange("l (r d) -> (l r) d", d=HD)).then_inc(prm_in, 16)
                e.dma_start(brow[0:3 * KB, :], b_ada[l].rearrange("(r d) -> r d", d=HD)).then_inc(prm_in, 16)
                e.dma_start(brow[3 * KB:N_BIAS, :], g_final.rearrange("(r d) -> r d", d=HD)).then_inc(prm_in, 16)
                e.dma_start(gw[:], w_in[l].rearrange("(k p) n -> p k n", p=P)[:, :, COL_GATES:COL_GATES + 2 * H_ML]
                            ).then_inc(gates_in, 16)
                e.dma_start(gb[0:H_ML, 0:1], b_i[l].rearrange("(h a) -> h a", a=1)).then_inc(gates_in, 16)
                e.dma_start(gb[0:H_ML, 1:2], b_f[l].rearrange("(h a) -> h a", a=1)).then_inc(gates_in, 16)
                e.dma_start(m6[:], st_m[l].rearrange("b h -> h b"), allow_slow_non_contiguous=True).then_inc(gates_in, 16)
                e.dma_start(conv_s[l, :, 0:PAD - 1, :], st_conv[l, :, 1:PAD, :]).then_inc(stored, 16)
                L0 = l * STORES_PER_LAYER + 1
                state = {"hg": (st_hg, hg_s), "ml": (st_c, c_s), "rt": (st_rt, rt_s)}
                n0 = L0
                for count, base, kind, _cols in GROUPS:
                    per = STORES[kind]
                    src, dst = state[kind]
                    if kind == "rt":
                        e.wait_ge(head_done, l * NH + base + 1)
                        held(e)
                        e.dma_start(rope_t, rope_d).then_inc(aux_in, 16)
                    with e.Fori(0, count) as i:
                        g = i + (l * NH + base)
                        e.wait_ge(stored, (i * per + n0) * 16)
                        e.wait_ge(head_done, g + 1)
                        held(e)
                        e.dma_start(ss[:], src[l, :, bass.ds(i, 1)].rearrange("b h k v -> k (b h) v")).then_inc(state_in, 16)
                        if kind == "rt":
                            e.dma_start(hc, hc_d[bass.ds(i, 1)].rearrange("h p n -> (h p) n")).then_inc(aux_in, 16)
                        if kind == "ml":
                            e.dma_start(selh[:], sel_d[bass.ds(i, 1)].rearrange("h p n -> (h p) n")).then_inc(aux_in, 16)
                            for j in range(2):
                                e.dma_start(cvr[:, j, :], st_conv[l, :, :, bass.ds(i * HD + j * W_ML, HD)]
                                            .rearrange("b r d -> (b r) d")).then_inc(aux_in, 16)
                            e.dma_start(nr[:], st_n[l, :, bass.ds(i, 1)].rearrange("b h d -> (b h) d")).then_inc(aux_in, 16)
                            n = i + l * H_ML
                            e.wait_ge(as_["cvo"], n + 1)
                            held(e)
                            for j in range(2):
                                cols = bass.ds(i * HD + j * W_ML, HD)
                                e.dma_start(conv_p[l, 0, :, cols], cvo[0:PAD, j, :]).then_inc(stored, 16)
                                e.dma_start(conv_s[l, :, PAD - 1, cols], cvo[PAD:PAD + NS, j, :]).then_inc(stored, 16)
                        e.wait_ge(vs["ss"], g + 1)
                        held(e)
                        e.dma_start(dst[l, :, bass.ds(i, 1)].rearrange("b h k v -> k (b h) v"), ss[:]).then_inc(stored, 16)
                        if kind == "ml":
                            e.wait_ge(vs["nrow"], n + 1)
                            held(e)
                            e.dma_start(n_s[l, :, bass.ds(i, 1)].rearrange("b h d -> (b h) d"), nr[:]).then_inc(stored, 16)
                            e.dma_start(n_p[l, 0, bass.ds(i, 1)].rearrange("h d -> d h"),
                                        st[:, NC - 1, HD:HD + 1],
                                        allow_slow_non_contiguous=True).then_inc(stored, 16)
                            e.wait_ge(as_["ct"], n + 1)
                            held(e)
                            e.dma_start(c_p[l, 0, bass.ds(i, 1)].rearrange("h v k -> (h v) k"), ct[:]).then_inc(stored, 16)
                        else:
                            e.wait_ge(vs["chain"], g + 1)
                            held(e)
                            out = hg_p if kind == "hg" else rt_p
                            e.dma_start(out[l, 0, bass.ds(i, 1)].rearrange("h k v -> (h k) v"),
                                        st[:, NC - 1, 0:HD]).then_inc(stored, 16)
                    n0 += per * count
                    if kind == "hg":
                        e.wait_ge(gsem["v2"], l + 1)
                        held(e)
                        e.dma_start(m_p[l].rearrange("b h -> h b"), g4[:, 3, NC - 1:NC], allow_slow_non_contiguous=True).then_inc(stored, 16)
                        e.dma_start(m_s[l].rearrange("b h -> h b"), g8[:, 3, :], allow_slow_non_contiguous=True).then_inc(stored, 16)
                        n0 += 2
            e.wait_ge(stored, DEPTH * STORES_PER_LAYER * 16)
            held(e)

        @block.tensor
        def _(e):
            def quarter(l, u, slot, par, part, src=None):
                act = h if src is None else src
                for kb in range(4 * part, 4 * part + 4):
                    for b in range(2):
                        last = e.matmul(pj[:, 2 * par + b, 0:HALF], ring[:, slot, kb * P:(kb + 1) * P],
                                        act[:, kb, b * HALF:(b + 1) * HALF], start=(kb == 0), stop=(kb == KB - 1))
                return last

            def tr(out, src, n):
                return e.transpose(out, src, cst[0:n, C_ID:C_ID + n])

            e.wait_ge(const_in, 16)
            e.wait_ge(silu_c, 1)
            for kb in range(KB):
                last = tr(mx[:, 2, kb * 9:kb * 9 + 9], crow[:, kb * P:(kb + 1) * P], 9)
            last.then_inc(sct_ready, 1)
            e.wait_ge(x_in, 64)
            for kb in range(KB):
                last = tr(mx[:, 3, kb * NS:(kb + 1) * NS], srow[:, kb * P:(kb + 1) * P], NS)
            last.then_inc(sct_ready, 1)
            for kb in range(KB):
                if kb >= 4:
                    e.wait_ge(xt_taken, kb - 3)
                for b in range(4):
                    last = tr(pj[:, kb % 4, b * P:(b + 1) * P], xrow[:, b, kb * P:(kb + 1) * P], P)
                last.then_inc(xt_ready, 1)
            e.wait_ge(xt_taken, KB)
            e.wait_ge(sct_taken, 2)

            def norm(n):
                for kb in range(KB):
                    e.wait_ge(sq_ready, n * KB + kb + 1)
                    for b in range(2):
                        last = e.matmul(mx[:, b, 0:HALF], ones, (t1, t2)[kb % 2][:, b * HALF:(b + 1) * HALF],
                                        start=(kb == 0), stop=(kb == KB - 1))
                    last.then_inc(sq_used, 1)

            for l in range(DEPTH):
                u0 = l * USES
                if l:
                    e.wait_ge(out_added, l * KB)
                e.wait_ge(prm_in, (l + 1) * 128)
                tr(mx[:, 1, 0:N_PRM], prow[0:N_PRM, :], N_PRM)
                tr(mx[:, 1, 128:128 + N_BIAS], brow[0:N_BIAS, :], N_BIAS).then_inc(prm_tr, 1)

                def ada_columns(n):
                    e.wait_ge(ada_taken, l * ADA_GROUPS + n + 1)
                    for c in range(4):
                        last = e.matmul(mx[:, 0, (4 * n + c) * 9:(4 * n + c) * 9 + 9],
                                        (t1, t2)[n % 2][:, c * P:(c + 1) * P], ssum, start=True, stop=True)
                    last.then_inc(ada_sum, 1)

                for n in range(ADA_GROUPS):
                    if n >= 2:
                        e.wait_ge(ada_taken, l * ADA_GROUPS + n - 1)
                    for s in range(SLOTS):
                        e.wait_ge(w_in_s[s], 16 * (u0 + n + 1))
                        for j in range(4):
                            last = e.matmul(pj[32 * j:32 * j + 32, n % 2, :], sct[:, 4 * s + j, :],
                                            ring[:, s, j * ADA_N:(j + 1) * ADA_N], start=(s == 0), stop=(s == SLOTS - 1))
                        last.then_inc(w_used, 1)
                    if n:
                        ada_columns(n - 1)
                ada_columns(ADA_GROUPS - 1)
                e.wait_ge(mod_ready, l + 1)
                norm(l)

                def tile_wait(u, slot, g):
                    e.wait_ge(w_in_s[slot], (u + 1) * 16)
                    e.wait_ge(taken, g * 4 + (slot + 1))

                def whole(u, slot, g, between=()):
                    tile_wait(u, slot, g)
                    for part in range(4):
                        last = quarter(l, u, slot, slot % 2, part)
                        if part == 3:
                            last.then_inc(w_used, 1)
                        if part < len(between) and between[part]:
                            between[part]()

                e.wait_ge(hs_ready, l + 1)
                e.wait_ge(h_ready, (l + 1) * KB)
                for count, base, kind, _cols in GROUPS:
                    if kind == "ml":
                        e.wait_ge(gates_in, (l + 1) * 64)
                        e.wait_ge(head_done, l * NH + H_HG + 1)
                        for kb in range(KB):
                            for j in range(4):
                                w = gw[:, kb, (j % 2) * H_ML:(j % 2 + 1) * H_ML]
                                last = e.matmul(mx[32 * j:32 * j + H_ML, 0, 0:HALF], w,
                                                h[:, kb, (j // 2) * HALF:(j // 2 + 1) * HALF],
                                                start=(kb == 0), stop=(kb == KB - 1))
                        last.then_inc(gsem["proj"], 1)
                        e.wait_ge(gsem["v2"], l + 1)
                        for what in range(3):
                            for c in range(NC):
                                tr(mx[:, 1, (what * NC + c) * 8:(what * NC + c) * 8 + H_ML],
                                   lev[0:H_ML, 2 + what, c * CH:(c + 1) * CH], H_ML)
                        for what in range(3):
                            tr(mx[0:NS, 2, what * 8:what * 8 + H_ML], g8[:, what, :], H_ML)
                        e.matmul(mx[:, 3, 0:H_ML * NC], cst[0:H_ML, C_ONE:C_ONE + 128], lev[0:H_ML, 5, 0:H_ML * NC],
                                 start=True, stop=True)
                        e.matmul(mx[:, 3, 64:64 + H_ML * NS], cst[0:H_ML, C_ONE:C_ONE + 128],
                                 lev[0:H_ML, 5, 64:64 + H_ML * NS], start=True, stop=True).then_inc(gsem["tr"], 1)
                        e.wait_ge(gsem["col"], l + 1)

                    with e.Fori(0, count) as i:
                        g = i + (l * NH + base)
                        n = i + l * count
                        u = i + (u0 + ADA_GROUPS + base)

                        def sample_rows():
                            e.wait_ge(vs["qk"], g + 1)
                            for j, src in enumerate((x1 if kind == "hg" else q, k, v)):
                                s0 = PAD + T if (kind == "hg" and j == 0) else T
                                last = tr(mx[0:NS, 3, j * HD:(j + 1) * HD], src[:, s0:s0 + NS], P)
                            return last

                        def v_rows():
                            e.wait_ge(taken, ht(g, 2))
                            for c in range(NC):
                                tr(mx[:, 1, c * HD:(c + 1) * HD], v[:, c * CH:(c + 1) * CH], P)

                        def k_rows():
                            kw = dt if kind == "hg" else k
                            for c in range(NC):
                                tr(mx[:, 2, c * HD:(c + 1) * HD], kw[:, c * CH:(c + 1) * CH], P)

                        def rows():
                            if kind == "hg":
                                e.wait_ge(vs["kw"], n + 1)
                                e.wait_ge(vs["a"], g + 1)
                            else:
                                e.wait_ge(vs["qk"], g + 1)
                            v_rows()
                            k_rows()
                            sample_rows().then_inc(ps["tr"], 1)

                        def scores():
                            e.wait_ge(vs["qk"], g + 1)
                            if kind == "ml":
                                e.wait_ge(as_["cvc"], n + 1)
                                e.wait_ge(as_["cvo"], n + 1)
                                e.wait_ge(as_["dt"], n + 1)
                                e.wait_ge(vs["qd"], n + 1)
                            for c in range(NC):
                                last = e.matmul(mx[:, 0, c * CH:(c + 1) * CH], k[:, c * CH:(c + 1) * CH],
                                                q[:, c * CH:(c + 1) * CH], start=True, stop=True)
                            last.then_inc(ps["score"], 1)

                        def rot(j):
                            def run():
                                e.wait_ge(taken, ht(g, j))
                                src = (x0, x1)[j]
                                for b in range(2):
                                    last = e.matmul(mx[:, 2 * j + b, 0:HALF], cst[:, C_ROT:C_ROT + 128],
                                                    src[:, PAD + b * HALF:PAD + (b + 1) * HALF], start=True, stop=True)
                                last.then_inc(ps[("rot_q", "rot_k")[j]], 1)
                            return run

                        def level_scores(vs_range):
                            def run():
                                for lv in vs_range:
                                    if lv < 0:
                                        e.wait_ge(vs["qk"], g + 1)
                                    else:
                                        e.wait_ge(vs["lev"], n * LEVELS + (lv + 1))
                                    if lv >= 3:
                                        e.wait_ge(vs["pred"], n * (LEVELS + 1) + (lv - 2))
                                    bank = (lv + 1) % 4
                                    for c in range(NC):
                                        cs = slice(c * CH, (c + 1) * CH)
                                        if lv < 0:
                                            last = e.matmul(mx[:, bank, cs], k[:, cs], x1[:, PAD + c * CH:PAD + (c + 1) * CH],
                                                            start=True, stop=True)
                                        else:
                                            last = e.matmul(mx[:, bank, cs], lev[:, lv, cs], lev[:, lv, cs],
                                                            start=True, stop=True)
                                    last.then_inc(ps["score"], 1)
                            return run

                        def states_u():
                            e.wait_ge(vs["a"], g + 1)
                            e.wait_ge(as_["vt"], g + 1)
                            e.wait_ge(as_["kt"], g + 1)
                            e.wait_ge(as_["sr"], g + 1)
                            w = HD + 1 if kind == "ml" else HD
                            for c in range(NC):
                                last = e.matmul(mx[:, c // 2, (c % 2) * 129:(c % 2) * 129 + w], kt[:, c, :], vt[:, c, 0:w],
                                                start=True, stop=True)
                            last.then_inc(ps["u"], 1)
                            e.wait_ge(vs["blk"], g + 1)
                            lhs = sw[:] if kind == "ml" else sr[:, 1, :]
                            for b in range(2):
                                last = e.matmul(mx[:, 2 + b, :], lhs, big[0:NS, b * 512:(b + 1) * 512], start=True, stop=True)
                            last.then_inc(ps["outer"], 1)

                        def outputs():
                            e.wait_ge(vs["chain"], g + 1)
                            w = HD + 1 if kind == "ml" else HD
                            for c in range(NC):
                                out = mx[:, c // 2, (c % 2) * 129:(c % 2) * 129 + w]
                                last = e.matmul(out, a[:, c, :], vt[:, c, 0:w], start=True, stop=(c == 0))
                                if c:
                                    last = e.matmul(out, qd[:, c * CH:(c + 1) * CH], st[:, c - 1, 0:w], start=False, stop=True)
                            last.then_inc(ps["o"], 1)
                            e.wait_ge(vs["ss"], g + 1)
                            if kind == "ml":
                                for b in range(2):
                                    last = e.matmul(mx[:, 2 + b, :], cst[0:NS, C_ONE:C_ONE + 128],
                                                    lev[0:NS, b, :], start=True, stop=True)
                            else:
                                qs = x1[:, PAD + T:PAD + TOK] if kind == "hg" else q[:, T:TOK]
                                for b in range(2):
                                    last = e.matmul(mx[0:NS, 2 + b, :], qs,
                                                    ss[:, 4 * b:4 * b + 4, :].rearrange("p s v -> p (s v)"),
                                                    start=True, stop=True)
                            last.then_inc(ps["os"], 1)

                        def ml_os():
                            e.wait_ge(vs["osc"], n + 1)
                            tr(mx[0:NS, 2, 0:HD], sm[:, 40:48], P).then_inc(ps["ostr"], 1)
                            tr(mx[:, 3, 128:256], st[:, NC - 1, 0:HD], P).then_inc(ps["cback"], 1)

                        def back():
                            if kind == "ml":
                                e.wait_ge(as_["ct"], n + 1)
                            e.wait_ge(vs["ho"], g + 1)
                            for c in range(NC):
                                tr(mx[:, 2, c * CH:(c + 1) * CH], ho[:, c, :], P)
                            tr(mx[:, 3, 0:NS], ho[0:NS, NC, :], NS).then_inc(ps["back"], 1)

                        def ml_first():
                            e.wait_ge(head_done, g + 1)
                            e.wait_ge(aux_in, auxc(l, kind, i))
                            e.matmul(mx[:, 0, :], selh[:], r6, start=True, stop=True)
                            e.matmul(mx[:, 1, :], selh[:], iw6[:], start=True, stop=True)
                            for j in range(2):
                                last = tr(mx[:, 3, 24 * j:24 * j + 24], cvr[:, j, :], NS * PAD)
                            last.then_inc(ps["bcast"], 1)

                        def ml_conv():
                            e.wait_ge(taken, ht(g, 1))
                            for j, src in enumerate((x0, x1)):
                                last = tr(mx[0:PAD + NS, 2, j * HD:(j + 1) * HD], src[:, T:T + PAD + NS], P)
                            last.then_inc(ps["conv"], 1)

                        if kind == "rt":
                            whole(u, 0, g)
                            whole(u, 1, g)
                            whole(u, 2, g, (rot(0), None, rot(1)))
                            whole(u, 3, g, (lambda: (scores(), rows()), states_u, outputs))
                        elif kind == "ml":
                            whole(u, 0, g)
                            whole(u, 1, g, (ml_first,))
                            whole(u, 2, g, (ml_conv,))
                            whole(u, 3, g, (lambda: (scores(), rows()), states_u, outputs, ml_os))
                        else:
                            whole(u, 0, g)
                            whole(u, 1, g)
                            whole(u, 2, g, (None, None, None, level_scores((-1, 0, 1, 2))))
                            whole(u, 3, g, (level_scores((3, 4, 5, 6)), rows, states_u, outputs))
                        back()

                e.wait_ge(head_done, (l + 1) * NH + 1)
                for n in range(KB):
                    slot, u = n % SLOTS, u0 + ADA_GROUPS + NH + n // SLOTS
                    e.wait_ge(w_in_s[slot], 16 * (u + 1))
                    if n >= 2:
                        e.wait_ge(out_added, l * KB + n - 1)
                    else:
                        e.wait_ge(taken, (l + 1) * NH * 4 + 2)
                    for part in range(4):
                        last = quarter(l, u, slot, n % 2, part, o)
                    last.then_inc(w_used, 1)
            e.wait_ge(out_added, DEPTH * KB)
            norm(DEPTH)
            for b in range(4):
                for m in range(4):
                    i = 4 * b + m
                    e.wait_ge(fin_n, 4 * m + 4 if b == 0 else KB)
                    if i >= 4:
                        e.wait_ge(fin_e, i - 3)
                    for c in range(4):
                        last = tr(pj[:, i % 4, c * P:(c + 1) * P], h[:, 4 * m + c, b * P:(b + 1) * P], P)
                    last.then_inc(fin_t, 1)
            e.wait_ge(rs_ready, 1)
            for kb in range(KB):
                last = tr(mx[0:NS, kb // 4, (kb % 4) * P:(kb % 4 + 1) * P], h[:, kb, T:TOK], P)
            last.then_inc(fin_t, 1)

        @block.scalar
        def _(e):
            def act(out, in_, func, **kw):
                return e.activation(out, in_, func, **kw)

            e.wait_ge(x_in, 64)
            act(e_row, crow, ACT.Exp, scale=-1.0).then_inc(c_exp, 1)
            e.drain().then_inc(taken, 2)
            e.wait_ge(sct_ready, 1)
            e.wait_ge(init_done, 1)
            act(sct[:, :, 0:9], mx[:, 2, 0:9 * KB].rearrange("p (k s) -> p k s", s=9), ACT.Copy).then_inc(sct_taken, 1)
            e.wait_ge(sct_ready, 2)
            act(y[:, :, T:TOK], mx[:, 3, 0:NS * KB].rearrange("p (k s) -> p k s", s=NS), ACT.Copy).then_inc(sct_taken, 1)
            for kb in range(KB):
                e.wait_ge(xt_ready, kb + 1)
                act(y[:, kb, 0:T], pj[:, kb % 4, :], ACT.Copy).then_inc(xt_taken, 1)

            def norm(n):
                for kb in range(KB):
                    if n * KB + kb >= 2:
                        e.wait_ge(sq_used, n * KB + kb - 1)
                    act((t1, t2)[kb % 2][:], y[:, kb, :], ACT.Square).then_inc(sq_ready, 1)
                e.wait_ge(ms_ready, n + 1)
                act(t3[:], t3[:], ACT.Ln)
                e.drain()
                act(t3[:], t3[:], ACT.Exp, scale=-0.5).then_inc(rs_made, 1)

            for l in range(DEPTH):
                e.wait_ge(prm_tr, l + 1)
                act(prm[:], mx[:, 1, 0:N_PRM], ACT.Copy).then_inc(prm_taken, 1)
                act(bia[:], mx[:, 1, 128:128 + N_BIAS], ACT.Copy).then_inc(prm_taken, 1)
                for n in range(ADA_GROUPS):
                    e.wait_ge(w_used, (l * USES + n + 1) * SLOTS)
                    if n >= 2:
                        e.wait_ge(ada_sum, l * ADA_GROUPS + n - 1)
                    act((t1, t2)[n % 2][:, 0:512], pj[:, n % 2, :], ACT.Copy).then_inc(ada_taken, 1)
                e.wait_ge(mod_ready, l + 1)
                if l:
                    e.wait_ge(lb_diff, 1)
                    act(lbc[:, 2, :], lbc[:, 2, :], ACT.Exp, scale=-1.0)
                    e.drain()
                    act(lbc[:, 2, :], lbc[:, 2, :], ACT.Ln, bias=1.0).then_inc(lb_ln, 1)
                norm(l)
                for kb in range(KB):
                    e.wait_ge(hn_ready, l * KB + kb + 1)
                    act(h[:, kb, 0:T], h[:, kb, 0:T], ACT.Identity, bias=mod[:, kb, 0:1]).then_inc(h_ready, 1)

                for count, base, kind, _cols in GROUPS:
                    if kind == "ml":
                        e.wait_ge(gsem["proj"], l + 1)
                        for b in range(2):
                            act(t1[0:H_ML, b * HALF:(b + 1) * HALF],
                                mx[64 * b:64 * b + H_ML, 0, 0:HALF], ACT.Identity, bias=gb[0:H_ML, 0:1])
                            act(t2[0:H_ML, b * HALF:(b + 1) * HALF],
                                mx[64 * b + 32:64 * b + 32 + H_ML, 0, 0:HALF], ACT.Identity, bias=gb[0:H_ML, 1:2])
                        e.drain()
                        act(t3[0:H_ML, :], t2[0:H_ML, :], ACT.Abs)
                        e.drain()
                        act(t3[0:H_ML, :], t3[0:H_ML, :], ACT.Exp, scale=-1.0)
                        e.drain()
                        act(t3[0:H_ML, :], t3[0:H_ML, :], ACT.Ln, bias=1.0).then_inc(gsem["a1"], 1)
                        e.wait_ge(gsem["v1"], l + 1)
                        act(iw6[:], iw6[:], ACT.Exp)
                        act(lev[0:H_ML, 3, :], lev[0:H_ML, 3, :], ACT.Exp)
                        act(lev[0:H_ML, 4, :], lev[0:H_ML, 4, :], ACT.Exp, scale=-1.0)
                        act(g4[:, 2, :], g4[:, 2, :], ACT.Exp)
                        act(g8[:, 0:2, :], g8[:, 4:6, :], ACT.Exp)
                        act(g8[:, 2, :], g8[:, 3, :], ACT.Exp, scale=-1.0).then_inc(gsem["a2"], 1)

                    with e.Fori(0, count) as i:
                        g = i + (l * NH + base)
                        n = i + l * count

                        def take(j, dst, off, scale=1.0):
                            e.wait_ge(w_used, i * SLOTS + ((l * USES + ADA_GROUPS + base) * SLOTS + j + 1))
                            for b in range(2):
                                last = act(dst[:, off + b * HALF:off + (b + 1) * HALF], pj[:, 2 * (j % 2) + b, 0:HALF],
                                           ACT.Copy, scale=scale)
                            last.then_inc(taken, 1)

                        def rows(scaled):
                            e.wait_ge(ps["tr"], g + 1)
                            act(vt[:, :, 0:HD], mx[:, 1, :].rearrange("p (c d) -> p c d", c=NC), ACT.Copy).then_inc(as_["vt"], 1)
                            if scaled == "ml":
                                e.wait_ge(vs["r"], n + 1)
                                for c in range(NC):
                                    last = act(kt[:, c, :], mx[:, 2, c * HD:(c + 1) * HD], ACT.Copy, scale=sm[:, 4 + c:5 + c])
                            else:
                                last = act(kt[:], mx[:, 2, :].rearrange("p (c d) -> p c d", c=NC), ACT.Copy,
                                           scale=hc[:, HC_ST:HC_ST + 1] if scaled == "rt" else 1.0)
                            last.then_inc(as_["kt"], 1)
                            act(sr[:], mx[0:NS, 3, 0:3 * HD].rearrange("p (j d) -> p j d", j=3), ACT.Copy).then_inc(as_["sr"], 1)

                        def z_exp():
                            act(t4[:], z[:], ACT.Exp, scale=-1.0).then_inc(as_["z"], 1)

                        e.wait_ge(head_done, g + 1)
                        if kind == "rt":
                            take(0, x0, PAD)
                            take(1, x1, PAD, SCALE)
                            take(2, v, 0)
                            e.wait_ge(aux_in, auxc(l, kind, i))
                            rows("rt")
                        elif kind == "ml":
                            take(0, x0, PAD)
                            e.wait_ge(ps["bcast"], n + 1)
                            act(cvc[:], mx[:, 3, 0:48].rearrange("p (j r) -> p j r", j=2), ACT.Copy).then_inc(as_["cvc"], 1)
                            e.wait_ge(vs["r"], n + 1)
                            act(dt[:], dt[:], ACT.Exp).then_inc(as_["dt"], 1)
                            e.wait_ge(vs["conv_q"], n + 1)
                            act(t3[:], t1[:], ACT.Exp, scale=-1.0).then_inc(as_["silu"], 1)
                            take(1, x1, PAD)
                            e.wait_ge(ps["conv"], n + 1)
                            act(cvo[:], mx[0:PAD + NS, 2, 0:2 * HD].rearrange("p (j d) -> p j d", j=2), ACT.Copy).then_inc(as_["cvo"], 1)
                            e.wait_ge(vs["conv_k"], n + 1)
                            act(t4[:], t2[:], ACT.Exp, scale=-1.0).then_inc(as_["silu"], 1)
                            take(2, v, 0)
                            rows("ml")
                        else:
                            take(0, x0, PAD)
                            f = x0[:, PAD:PAD + TOK]
                            e.drain()
                            act(t1[:], f, ACT.Abs)
                            e.drain()
                            act(t1[:], t1[:], ACT.Exp, scale=-1.0)
                            e.drain()
                            act(t1[:], t1[:], ACT.Ln, bias=1.0).then_inc(as_["l1"], 1)
                            e.wait_ge(vs["d1"], n + 1)
                            act(k[:], t4[:], ACT.Exp, bias=sm[:, 9:10]).then_inc(as_["kk"], 1)
                            act(t3[:], t3[:], ACT.Exp, scale=-1.0)
                            e.drain()
                            act(t3[:], t3[:], ACT.Ln, bias=1.0).then_inc(as_["l2"], 1)
                            take(1, x1, PAD, SCALE)
                            e.wait_ge(vs["b"], n + 1)
                            act(qd[:], t2[:, 0:T], ACT.Exp)
                            act(sm[:, 16:20], t2[:, CH - 1:T:CH], ACT.Exp)
                            act(sm[:, 24:32], t3[:, T:TOK], ACT.Exp)
                            act(dt[:], t4[:, 0:T], ACT.Exp, scale=-1.0).then_inc(as_["eb"], 1)
                            for lv in range(LEVELS):
                                e.wait_ge(vs["lf"], n * LEVELS + (lv + 1))
                                x = 64 >> lv
                                w = lev[:, lv, :].rearrange("p (n s x) -> p n s x", s=2, x=x)
                                act(w[:, :, 0, :], w[:, :, 0, :], ACT.Exp, scale=-1.0)
                                act(w[:, :, 1, :], w[:, :, 1, :], ACT.Exp).then_inc(as_["lev"], 1)
                            take(2, v, 0)
                            rows("hg")
                        take(3, z, 0)
                        e.drain()
                        e.wait_ge(vs["a"], g + 1)
                        z_exp()
                        if kind == "ml":
                            e.wait_ge(ps["cback"], n + 1)
                            act(ct[:], mx[:, 3, 128:256], ACT.Copy).then_inc(as_["ct"], 1)
                        e.wait_ge(vs["var"], g + 1)
                        act(rstd[:], bag[:, :, 1], ACT.Ln)
                        e.drain()
                        act(rstd[:], rstd[:], ACT.Exp, scale=-0.5).then_inc(as_["rs"], 1)
            e.wait_ge(out_added, DEPTH * KB)
            norm(DEPTH)
            for i in range(16):
                e.wait_ge(fin_t, i + 1)
                act(yrow[:, i // 4, (i % 4) * 512:(i % 4 + 1) * 512], pj[:, i % 4, :], ACT.Copy).then_inc(fin_e, 1)
            e.wait_ge(fin_t, 17)
            for b in range(4):
                act(ysrow[:, b * 512:(b + 1) * 512], mx[0:NS, b, :], ACT.Copy).then_inc(fin_e, 1)

        @block.vector
        def _(e):
            def tt(out, a_, b_, op):
                return e.tensor_tensor(out, a_, b_, op)

            def ts(out, a_, s1, s2, op0, op1=None):
                return e.tensor_scalar(out, a_, s1, s2, op0, op1) if op1 is not None else e.tensor_scalar(out, a_, s1, None, op0)

            def stt(out, a_, s, b_, op0, op1):
                return e.scalar_tensor_tensor(out=out, in0=a_, scalar=s, in1=b_, op0=op0, op1=op1)

            def bc(ap, axis, n):
                return ap.unsqueeze(axis).broadcast_to([*ap.shape[:axis], n, *ap.shape[axis:]])

            def absolute(out, a_):
                return stt(out, a_, -1.0, a_, ALU.mult, ALU.max)

            M, A_, S_, MAX, MIN = ALU.mult, ALU.add, ALU.subtract, ALU.max, ALU.min

            e.memset(sct[:], 0.0)
            e.memset(x0[:, 0:PAD], 0.0)
            e.memset(x1[:, 0:PAD], 0.0)
            e.memset(vt[:, :, HD:HD + 1], 1.0)
            e.memset(g4[:], 0.0)
            e.memset(bag[:], 1.0)
            e.drain().then_inc(init_done, 1)
            e.sem_inc(head_done, 1)
            e.wait_ge(c_exp, 1)
            ts(e_row, e_row, 1.0, None, A_)
            e.drain()
            e.reciprocal(e_row, e_row)
            e.drain()
            tt(crow, crow, e_row, M).then_inc(silu_c, 1)

            def norm(n, last=False):
                e.wait_ge(sq_used, (n + 1) * KB)
                for b in range(2):
                    ts(t3[:, b * HALF:(b + 1) * HALF], mx[:, b, 0:HALF], 1.0 / D, EPS, M, A_)
                e.drain().then_inc(ms_ready, 1)
                e.wait_ge(rs_made, n + 1)

            for l in range(DEPTH):
                e.wait_ge(ada_sum, (l + 1) * ADA_GROUPS)
                e.wait_ge(prm_taken, 2 * (l + 1))
                tt(mod[:], mx[:, 0, 0:27 * KB].rearrange("p (k s) -> p k s", s=9), bc(bia[:, 0:3 * KB], 2, 9), A_)
                e.drain()
                stt(ag[:], mod[:, KB:2 * KB, :], 1.0, bc(prm[:, R_NORM:R_NORM + KB], 2, 9), A_, M).then_inc(mod_ready, 1)
                lb0, lb1 = prm[:, R_LB:R_LB + H_HG], prm[:, R_LB + H_HG:R_LB + 2 * H_HG]
                if l == 0:
                    e.memset(lbc[:, 0, :], -1e30)
                    e.memset(lbc[:, 1, :], 0.0)
                else:
                    tt(lbc[:, 2, :], lb0, lb1, S_)
                    tt(sm[:, 0:4], lb0, lb1, MAX)
                    e.drain()
                    absolute(lbc[:, 2, :], lbc[:, 2, :])
                    tt(sm[:, 4:8], lb1, sm[:, 0:4], S_)
                    tt(sm[:, 8:12], lb0, sm[:, 0:4], S_)
                    e.drain().then_inc(lb_diff, 1)
                    e.wait_ge(lb_ln, 1)
                    tt(lbc[:, 0, :], sm[:, 4:8], lbc[:, 2, :], S_)
                    tt(lbc[:, 1, :], sm[:, 8:12], lbc[:, 2, :], S_)
                norm(l)
                for kb in range(KB):
                    stt(h[:, kb, 0:T], y[:, kb, 0:T], ag[:, kb, 0:1], t3[:, 0:T], M, M).then_inc(hn_ready, 1)
                hs = h[:, :, T:TOK]
                tt(hs, y[:, :, T:TOK], bc(t3[:, T:TOK], 1, KB), M)
                e.drain()
                tt(hs, hs, ag[:, :, 1:9], M)
                e.drain()
                tt(hs, hs, mod[:, 0:KB, 1:9], A_).then_inc(hs_ready, 1)

                for count, base, kind, _cols in GROUPS:
                    if kind == "ml":
                        G = slice(0, H_ML)
                        e.wait_ge(gsem["a1"], l + 1)
                        ig, fg = t1[G, :], t2[G, :]
                        b6, m_, u6 = lev[G, 0, :], lev[G, 1, :], lev[G, 2, :]
                        stt(fg, fg, 0.0, t3[G, :], MIN, S_)
                        e.drain()
                        e.tensor_tensor_scan(b6, cst[G, C_RST:C_RST + T], fg[:, 0:T], 0.0, M, A_)
                        e.tensor_tensor_scan(m_, fg[:, 0:T], ig[:, 0:T], 0.0, A_, MAX)
                        tt(g8[:, 6, :], fg[:, T:TOK], m6[:], A_)
                        e.drain()
                        tt(g8[:, 3, :], g8[:, 6, :], ig[:, T:TOK], MAX)
                        tt(r6, b6, m_, S_)
                        tt(u6, ig[:, 0:T], b6, S_)
                        e.tensor_copy(g4[:, 0, 1:NC], m_[:, CH - 1:T - 1:CH])
                        e.tensor_copy(g4[:, 3, :], m_[:, CH - 1:T:CH])
                        e.drain()
                        tt(g8[:, 4, :], g8[:, 6, :], g8[:, 3, :], S_)
                        tt(g8[:, 5, :], ig[:, T:TOK], g8[:, 3, :], S_)
                        e.tensor_copy(g4[:, 1, :], r6[:, CH - 1:T:CH])
                        e.drain()
                        tt(g4[:, 2, :], g4[:, 1, :], g4[:, 0, :], A_)
                        tt(iw6[:].rearrange("p (c t) -> p c t", c=NC), r6.rearrange("p (c t) -> p c t", c=NC),
                           bc(g4[:, 0, :], 2, CH), A_)
                        tt(lev[G, 3, :].rearrange("p (c t) -> p c t", c=NC), u6.rearrange("p (c t) -> p c t", c=NC),
                           bc(g4[:, 1, :], 2, CH), A_)
                        e.tensor_copy(lev[G, 4, :], m_)
                        e.drain().then_inc(gsem["v1"], 1)
                        e.wait_ge(gsem["a2"], l + 1)
                        tt(lev[G, 5, 0:H_ML * NC].rearrange("p (h c) -> p h c", c=NC), bc(g4[:, 2, :], 1, H_ML),
                           bc(cst[G, C_ID:C_ID + H_ML], 2, NC), M)
                        tt(lev[G, 5, 64:64 + H_ML * NS].rearrange("p (h c) -> p h c", c=NS), bc(g8[:, 0, :], 1, H_ML),
                           bc(cst[G, C_ID:C_ID + H_ML], 2, NS), M)
                        e.drain().then_inc(gsem["v2"], 1)
                        e.wait_ge(gsem["tr"], l + 1)
                        e.tensor_copy(gcol[:, :, 0:3, :].rearrange("p h w c -> p w c h"),
                                      mx[:, 1, 0:96].rearrange("p (w c x) -> p w c x", w=3, x=8)[:, :, :, 0:H_ML])
                        e.tensor_copy(gcol[:, :, 3, :], mx[:, 3, 0:H_ML * NC].rearrange("p (h c) -> p h c", c=NC))
                        e.tensor_copy(gs[:].rearrange("p h w -> p w h"),
                                      mx[0:NS, 2, 0:24].rearrange("p (w x) -> p w x", x=8)[:, :, 0:H_ML])
                        e.tensor_copy(gsb[:], mx[:, 3, 64:64 + H_ML * NS].rearrange("p (h s) -> p h s", s=NS))
                        e.drain().then_inc(gsem["col"], 1)

                    with e.Fori(0, count) as i:
                        g = i + (l * NH + base)
                        n = i + l * count

                        def gain():
                            e.tensor_copy(sm[:, 32:33], prm[:, bass.ds(i + (R_GN + base), 1)])

                        def blocks(src, dst):
                            tt(dst.rearrange("p (s d) -> p s d", s=NS), bc(src, 1, NS),
                               bc(cst[0:NS, C_ID:C_ID + NS], 2, HD), M)

                        def rope(j, dst):
                            e.wait_ge(ps[("rot_q", "rot_k")[j]], n + 1)
                            tt(dst[:], (x0, x1)[j][:, PAD:PAD + TOK], rope_t[:, 0:TOK], M)
                            for b in range(2):
                                tt(t1[:, b * HALF:(b + 1) * HALF], mx[:, 2 * j + b, 0:HALF],
                                   rope_t[:, TOK + b * HALF:TOK + (b + 1) * HALF], M)
                            e.drain()
                            tt(dst[:], dst[:], t1[:], A_)
                            e.drain()

                        def conv(j, dst, name):
                            src = (x0, x1)[j]
                            w = [sm[:, 48 + 2 * m + j:49 + 2 * m + j] for m in range(CONV_W)]
                            cb = sm[:, 56 + j:57 + j]
                            old = cvc[:, j, :].rearrange("p (s r) -> p s r", r=PAD)
                            ts(dst[:, 0:T], src[:, 0:T], w[0], cb, M, A_)
                            ts(dst[:, T:TOK], old[:, :, 0], w[0], cb, M, A_)
                            for m in range(1, CONV_W):
                                e.drain()
                                stt(dst[:, 0:T], src[:, m:m + T], w[m], dst[:, 0:T], M, A_)
                                x = old[:, :, m] if m < PAD else src[:, PAD + T:PAD + TOK]
                                stt(dst[:, T:TOK], x, w[m], dst[:, T:TOK], M, A_)
                            e.drain().then_inc(vs[name], 1)

                        if kind == "rt":
                            gain()
                            e.wait_ge(aux_in, auxc(l, kind, i))
                            rope(0, q)
                            tt(qd[:], q[:, 0:T], hc[:, HC_IN:HC_IN + T], M)
                            e.tensor_copy(sm[:, 16:20], hc[:, HC_CD:HC_CD + NC])
                            e.tensor_copy(sm[:, 24:32], hc[:, HC_G:HC_G + NS])
                            rope(1, k)
                            e.drain().then_inc(vs["qk"], 1)
                            e.wait_ge(ps["score"], scorec(l, kind, i, 1))
                            tt(a[:], mx[:, 0, :].rearrange("p (c t) -> p c t", c=NC), bc(hc[:, HC_D:HC_D + CH], 1, NC),
                               M)
                            e.drain().then_inc(vs["a"], 1)
                        elif kind == "ml":
                            gain()
                            e.tensor_copy(sm[:, 33:34], prm[:, bass.ds(i + R_SKIP, 1)])
                            for m in range(2 * CONV_W):
                                e.tensor_copy(sm[:, 48 + m:49 + m], prm[:, bass.ds(i + (R_CW + m * H_ML), 1)])
                            for j in range(2):
                                e.tensor_copy(sm[:, 56 + j:57 + j], prm[:, bass.ds(i + (R_CB + j * H_ML), 1)])
                            gh = gcol[:, bass.ds(i, 1)].rearrange("p h w c -> p (h w) c")
                            e.tensor_copy(sm[:, 0:8].rearrange("p (w c) -> p w c", w=2), gh[:, 0:2, :])
                            e.tensor_copy(sm[:, 12:20].rearrange("p (w c) -> p w c", w=2), gh[:, 2:4, :])
                            e.tensor_copy(sm[:, 24:32], gsb[:, bass.ds(i, 1)].rearrange("p h s -> p (h s)"))
                            e.tensor_copy(sm[0:NS, 60:63], gs[:, bass.ds(i, 1)].rearrange("p h w -> p (h w)"))
                            e.drain()
                            e.wait_ge(ps["bcast"], n + 1)
                            tt(dt[:].rearrange("p (c t) -> p c t", c=NC), mx[:, 0, :].rearrange("p (c t) -> p c t", c=NC),
                               bc(sm[:, 0:4], 2, CH), A_)
                            e.tensor_copy(lev[:, 2, :], mx[:, 1, :])
                            e.drain()
                            tt(dt[:].rearrange("p (c t) -> p c t", c=NC), dt[:].rearrange("p (c t) -> p c t", c=NC),
                               bc(cst[:, C_NEG:C_NEG + 128], 1, NC), A_)
                            e.drain().then_inc(vs["r"], 1)
                            e.wait_ge(taken, ht(g, 0))
                            e.wait_ge(as_["cvc"], n + 1)
                            conv(0, t1, "conv_q")
                            e.wait_ge(as_["silu"], 2 * n + 1)
                            ts(t3[:], t3[:], 1.0, None, A_)
                            e.drain()
                            e.reciprocal(t3[:], t3[:])
                            e.drain()
                            tt(q[:], t1[:], t3[:], M)
                            e.wait_ge(taken, ht(g, 1))
                            conv(1, t2, "conv_k")
                            e.wait_ge(as_["silu"], 2 * n + 2)
                            ts(t4[:], t4[:], 1.0, None, A_)
                            tt(qd[:], q[:, 0:T], lev[:, 2, :], M)
                            e.drain()
                            e.reciprocal(t4[:], t4[:])
                            e.drain().then_inc(vs["qd"], 1)
                            e.drain()
                            stt(k[:], t2[:], SCALE, t4[:], M, M)
                            e.drain().then_inc(vs["qk"], 1)
                            e.wait_ge(ps["score"], scorec(l, kind, i, 1))
                            tt(a[:].rearrange("p c t -> p (c t)"), mx[:, 0, :], dt[:], M)
                            e.drain().then_inc(vs["a"], 1)
                        else:
                            gain()
                            e.tensor_copy(sm[:, 8:9], lbc[:, 0, bass.ds(i, 1)])
                            e.tensor_copy(sm[:, 9:10], lbc[:, 1, bass.ds(i, 1)])
                            e.drain()
                            e.wait_ge(as_["l1"], n + 1)
                            f = x0[:, PAD:PAD + TOK]
                            stt(t2[:], f, 0.0, t1[:], MIN, S_)
                            e.drain()
                            tt(t4[:], t2[:], f, S_)
                            ts(t3[:], t2[:], sm[:, 9:10], sm[:, 8:9], A_, S_)
                            e.drain()
                            absolute(t3[:], t3[:])
                            ts(t2[:], t2[:], sm[:, 9:10], sm[:, 8:9], A_, MAX)
                            e.drain().then_inc(vs["d1"], 1)
                            e.wait_ge(as_["l2"], n + 1)
                            tt(t3[:], t2[:], t3[:], A_)
                            e.drain()
                            e.tensor_tensor_scan(t2[:, 0:T], cst[:, C_RST:C_RST + T], t3[:, 0:T], 0.0, M, A_)
                            e.drain()
                            bb = t2[:, 0:T].rearrange("p (c t) -> p c t", c=NC)
                            tt(t4[:, 0:T].rearrange("p (c t) -> p c t", c=NC), bb,
                               bc(t2[:, CH - 1:T:CH], 2, CH), S_)
                            e.drain().then_inc(vs["b"], 1)
                            for lv in range(LEVELS):
                                x = 64 >> lv
                                nb = T // (2 * x)
                                src = t2[:, 0:T].rearrange("p (n y) -> p n y", y=2 * x)
                                tt(lev[:, lv, :].rearrange("p (n y) -> p n y", y=2 * x), src,
                                   src[:, :, x - 1:x].broadcast_to([P, nb, 2 * x]), S_).then_inc(vs["lf"], 1)
                            e.wait_ge(taken, ht(g, 1))
                            e.wait_ge(as_["eb"], n + 1)
                            e.wait_ge(as_["kk"], n + 1)
                            e.sem_inc(vs["qk"], 1)
                            qq = x1[:, PAD:PAD + T]
                            tt(qd[:], qd[:], qq, M)
                            tt(dt[:], dt[:], k[:, 0:T], M)
                            e.drain().then_inc(vs["kw"], 1)
                            for lv in range(LEVELS):
                                e.wait_ge(as_["lev"], n * LEVELS + (lv + 1))
                                x = 64 >> lv
                                w = lev[:, lv, :].rearrange("p (n s x) -> p n s x", s=2, x=x)
                                kv = k[:, 0:T].rearrange("p (n s x) -> p n s x", s=2, x=x)
                                qv = qq.rearrange("p (n s x) -> p n s x", s=2, x=x)
                                tt(w[:, :, 0, :], w[:, :, 0, :], kv[:, :, 0, :], M)
                                tt(w[:, :, 1, :], w[:, :, 1, :], qv[:, :, 1, :], M)
                                e.drain().then_inc(vs["lev"], 1)
                            for lv in range(-1, LEVELS):
                                e.wait_ge(ps["score"], scorec(l, kind, i, lv + 2))
                                bank = mx[:, (lv + 1) % 4, :].rearrange("p (c t) -> p c t", c=NC)
                                if lv < 0:
                                    tt(a[:], bank, bc(ident, 1, NC), M)
                                else:
                                    held(e)
                                    mk = cst[:, C_LEV + 128 * lv:C_LEV + 128 * lv + 128].bitcast(U32)
                                    e.copy_predicated(a[:], bc(mk, 1, NC), bank)
                                e.drain().then_inc(vs["pred"], 1)
                            e.drain().then_inc(vs["a"], 1)

                        e.wait_ge(as_["sr"], g + 1)
                        if kind == "ml":
                            ts(sw[:], sr[:, 1, :], sm[0:NS, 61:62], None, M)
                            e.drain()
                            e.wait_ge(aux_in, auxc(l, kind, i))
                            stt(nr[:], nr[:], sm[0:NS, 60:61], sw[:], M, A_)
                            e.drain().then_inc(vs["nrow"], 1)
                            e.tensor_tensor_reduce(out=t1[0:NS, 0:HD], in0=nr[:], in1=sr[:, 0, :], scale=1.0, scalar=0.0,
                                                   op0=M, op1=A_, accum_out=sm[0:NS, 63:64])
                            ts(sw[:], sr[:, 2, :], sm[0:NS, 61:62], None, M)
                            blocks(sr[:, 1, :], big[0:NS, :])
                            blocks(sr[:, 0, :], lev[0:NS, 0:2, :].rearrange("p a b -> p (a b)"))
                        else:
                            blocks(sr[:, 2, :], big[0:NS, :])
                        e.drain().then_inc(vs["blk"], 1)
                        e.wait_ge(state_in, (g + 1) * 16)
                        e.wait_ge(ps["u"], g + 1)
                        w = HD + 1 if kind == "ml" else HD
                        for c in range(NC):
                            uc = mx[:, c // 2, (c % 2) * 129:(c % 2) * 129 + w]
                            if c == 0:
                                e.tensor_copy(st[:, 0, 0:w], uc)
                            else:
                                stt(st[:, c, 0:w], st[:, c - 1, 0:w], sm[:, 16 + c:17 + c], uc, M, A_)
                            e.drain()
                        e.drain().then_inc(vs["chain"], 1)
                        tt(ss[:], ss[:], bc(sm[:, 24:32], 2, HD), M)
                        e.drain()
                        e.wait_ge(ps["outer"], g + 1)
                        tt(ss[:].rearrange("p s v -> p (s v)"), ss[:].rearrange("p s v -> p (s v)"),
                           mx[:, 2:4, :].rearrange("p b n -> p (b n)"), A_)
                        e.drain().then_inc(vs["ss"], 1)

                        e.wait_ge(ps["o"], g + 1)
                        ov = mx[:, 0:2, 0:258].rearrange("p b (c d) -> p b c d", c=2)
                        hv = ho[:, 0:NC, :].rearrange("p (b c) d -> p b c d", b=2)
                        if kind == "ml":
                            den = sm[:, 34:38]
                            den4 = den.rearrange("p (b c) -> p b c", b=2)
                            e.tensor_copy(den4, ov[:, :, :, HD])
                            e.drain()
                            absolute(den, den)
                            e.drain()
                            tt(den, den, sm[:, 12:16], MAX)
                            e.drain()
                            e.reciprocal(den, den)
                            e.drain()
                            tt(hv, ov[:, :, :, 0:HD], den4.unsqueeze(3).broadcast_to([P, 2, 2, HD]), M)
                        else:
                            e.tensor_copy(hv, ov[:, :, :, 0:HD])
                        e.drain()
                        e.wait_ge(ps["os"], g + 1)
                        if kind == "ml":
                            qb = mx[:, 2:4, :].rearrange("p b n -> p (b n)")
                            tt(big, ss[:].rearrange("p s v -> p (s v)"), qb, M)
                            e.drain()
                            e.reduce_sum(sm[:, 40:48], big.rearrange("p (s d) -> p s d", s=NS), axis=mybir.AxisListType.X)
                            absolute(sm[0:NS, 63:64], sm[0:NS, 63:64])
                            e.drain().then_inc(vs["osc"], 1)
                            tt(sm[0:NS, 63:64], sm[0:NS, 63:64], sm[0:NS, 62:63], MAX)
                            e.drain()
                            e.reciprocal(sm[0:NS, 63:64], sm[0:NS, 63:64])
                            e.drain()
                            e.wait_ge(ps["ostr"], n + 1)
                            ts(ho[0:NS, NC, :], mx[0:NS, 2, 0:HD], sm[0:NS, 63:64], None, M)
                        else:
                            tt(big[0:NS, :].rearrange("p (s d) -> p s d", s=NS),
                               mx[0:NS, 2:4, :].rearrange("p b (s d) -> p (b s) d", d=HD),
                               bc(cst[0:NS, C_ID:C_ID + NS], 2, HD), M)
                            e.drain()
                            e.reduce_sum(ho[0:NS, NC, :], big[0:NS, :].rearrange("p (s d) -> p d s", s=NS),
                                         axis=mybir.AxisListType.X)
                        e.drain()
                        for c in range(NC + 1):
                            r = slice(0, P if c < NC else NS)
                            e.bn_stats(bst[r, c, :], ho[r, c, :])
                        e.drain()
                        for c in range(NC + 1):
                            r = slice(0, P if c < NC else NS)
                            e.bn_aggr(bag[r, c, :], bst[r, c, :])
                        e.drain()
                        for r, cs in ((slice(0, P), slice(0, NC)), (slice(0, NS), slice(NC, NC + 1))):
                            mean, var = bag[r, cs, 0], bag[r, cs, 1]
                            if kind == "hg":
                                tt(mean, mean, mean, M)
                                e.drain()
                                tt(var, var, mean, A_)
                                e.drain()
                            ts(var, var, EPS, None, A_)
                        e.drain().then_inc(vs["var"], 1)
                        e.wait_ge(as_["z"], g + 1)
                        ts(t4[:], t4[:], 1.0, None, A_)
                        e.drain()
                        e.reciprocal(t4[:], t4[:])
                        e.drain()
                        tt(z[:], z[:], t4[:], M)
                        e.wait_ge(as_["rs"], g + 1)
                        for c in range(NC + 1):
                            r = slice(0, P if c < NC else NS)
                            if kind == "hg":
                                ts(ho[r, c, :], ho[r, c, :], rstd[r, c:c + 1], None, M)
                            else:
                                ts(ho[r, c, :], ho[r, c, :], bag[r, c, 0:1], rstd[r, c:c + 1], S_, M)
                        e.drain().then_inc(vs["ho"], 1)
                        e.wait_ge(ps["back"], g + 1)
                        dst = o[:, bass.ds(i + base, 1), :].rearrange("p h t -> p (h t)")
                        if kind == "ml":
                            e.wait_ge(as_["ct"], n + 1)
                            ts(t2[:], q[:], sm[:, 33:34], None, M)
                            e.drain()
                            stt(t2[:, 0:T], mx[:, 2, :], sm[:, 32:33], t2[:, 0:T], M, A_)
                            stt(t2[:, T:TOK], mx[:, 3, 0:NS], sm[:, 32:33], t2[:, T:TOK], M, A_)
                            e.drain()
                            tt(dst, t2[:], z[:], M)
                        else:
                            stt(dst[:, 0:T], mx[:, 2, :], sm[:, 32:33], z[:, 0:T], M, M)
                            stt(dst[:, T:TOK], mx[:, 3, 0:NS], sm[:, 32:33], z[:, T:TOK], M, M)
                        e.drain().then_inc(head_done, 1)

                for n in range(KB):
                    e.wait_ge(w_used, (l * USES + ADA_GROUPS + NH) * SLOTS + n + 1)
                    gt = mod[:, 2 * KB + n, :]
                    p0, p1 = pj[:, 2 * (n % 2), 0:HALF], pj[:, 2 * (n % 2) + 1, 0:HALF]
                    stt(y[:, n, 0:HALF], p0, gt[:, 0:1], y[:, n, 0:HALF], M, A_)
                    stt(y[:, n, HALF:T], p1[:, 0:T - HALF], gt[:, 0:1], y[:, n, HALF:T], M, A_)
                    tt(sm[:, 0:NS], p1[:, T - HALF:HALF], gt[:, 1:9], M)
                    e.drain()
                    tt(y[:, n, T:TOK], y[:, n, T:TOK], sm[:, 0:NS], A_)
                    e.drain().then_inc(out_added, 1)
            norm(DEPTH)
            e.drain().then_inc(rs_ready, 1)
            for kb in range(KB):
                stt(h[:, kb, :], y[:, kb, :], bia[:, 3 * KB + kb:3 * KB + kb + 1], t3[:], M, M).then_inc(fin_n, 1)


_IN = ["x_prompt", "x_sample", "state_hgrn", "state_mlstm_C", "state_mlstm_n", "state_mlstm_m", "state_mlstm_conv",
       "state_ret", "c_prompt", "c_sample", "g_norm", "w_ada", "b_ada", "w_in", "hgrn_lb", "mlstm_conv_w",
       "mlstm_conv_b", "mlstm_b_i", "mlstm_b_f", "mlstm_skip", "w_gn", "w_out", "g_final"]


def _states(b):
    return [(DEPTH, b, H_HG, HD, HD), (DEPTH, b, H_ML, HD, HD), (DEPTH, b, H_ML, HD), (DEPTH, b, H_ML),
            (DEPTH, b, PAD, 2 * W_ML), (DEPTH, b, H_RT, HD, HD)]


_OUT = [(1, T, D), (NS, 1, D)] + _states(1) + _states(NS)


def kernel(**inputs):
    import concourse.bacc as bacc
    from concourse.bass_utils import run_bass_kernel_spmd as run

    nc = bacc.Bacc("TRN2", target_bir_lowering=False, num_devices=1)
    arrays, args = {}, []
    given = [(n, np.ascontiguousarray(inputs[n])) for n in _IN] + list(zip(("cst", "hc", "rope", "sel"), constants()))
    for name, arr in given:
        arrays["in_" + name] = arr
        args.append(nc.dram_tensor("in_" + name, arr.shape, mybir.dt.from_np(arr.dtype), kind="ExternalInput").ap())
    for i, shape in enumerate(_OUT):
        args.append(nc.dram_tensor(f"out_{i}", shape, F32, kind="ExternalOutput").ap())
    program(nc, *args)
    r = run(nc, [arrays], core_ids=[0])
    return tuple(r.results[0][f"out_{i}"] for i in range(len(_OUT)))
```

```python
from contextlib import ExitStack

import numpy as np
import concourse.bass as bass
from concourse import mybir

F32 = mybir.dt.float32
F32R = mybir.dt.float32r
U8 = mybir.dt.uint8
ALU = mybir.AluOpType
ACT = mybir.ActivationFunctionType

P = 128
DEPTH, D, T, NS, HD = 2, 2048, 512, 8, 128
KB = D // P
TOK = T + NS
HALF = TOK // 2
CH = 128
NC = T // CH
H_HG, H_ML, H_RT = 4, 6, 6
NH = H_HG + H_ML + H_RT
W_HG, W_ML, W_RT = H_HG * HD, H_ML * HD, H_RT * HD
COL_HG = (W_HG, 0, 2 * W_HG)
COL_ML = (3 * W_HG, 3 * W_HG + W_ML, 3 * W_HG + 2 * W_ML)
COL_GATES = 3 * W_HG + 3 * W_ML
COL_RT = tuple(COL_GATES + 2 * H_ML + j * W_RT for j in range(3))
COL_Z = COL_GATES + 2 * H_ML + 3 * W_RT
CONV_W = 4
PAD = CONV_W - 1
EPS = 1e-6
SCALE = HD ** -0.5
PAST = 4096
LEVELS = 7
ADA_N = 512
ADA_GROUPS = 3 * D // ADA_N
ADA_K = 2
ADA_PIECES = KB // ADA_K
RAW = 4
TILES = 4 * NH + KB

R_GN, R_SKIP, R_CW = 0, NH, NH + H_ML
R_CB = R_CW + CONV_W * 2 * H_ML
R_NORM = R_CB + 2 * H_ML
R_LB = R_NORM + KB
N_PRM = R_LB + DEPTH * H_HG
N_BIAS = 3 * KB + KB

C_ID, C_ROT, C_NEG = 0, 128, 256
C_SUM = 384
C_ONE = C_SUM + 9
N_CST = C_ONE + 128
HC_D, HC_IN, HC_ST, HC_CD, HC_G = 0, 128, 640, 641, 645
N_HC = 653


STORES = {"hg": 2, "ml": 8, "rt": 2}
STORES_PER_LAYER = 3 + sum(n * STORES[t] for n, t in ((H_HG, "hg"), (H_ML, "ml"), (H_RT, "rt")))


def constants():
    f = np.float32
    i = np.arange(128)
    c = np.zeros((128, N_CST), f)
    c[:, C_ID:C_ID + 128] = np.eye(128)
    for m in range(64):
        c[m + 64, C_ROT + m] = -1.0
        c[m, C_ROT + m + 64] = 1.0
    c[:, C_NEG:C_NEG + 128] = np.where(i[None, :] >= i[:, None], 0.0, -1e30)
    lm = np.zeros((128, LEVELS * 128), f)
    for v in range(LEVELS):
        h = 64 >> v
        same = i[:, None] // (2 * h) == i[None, :] // (2 * h)
        lm[:, 128 * v:128 * v + 128] = same & (i[:, None] // h % 2 == 0) & (i[None, :] // h % 2 == 1)
    inv = (f(10000.0) ** (-np.arange(64, dtype=f) / f(64))).astype(f)
    pos = np.concatenate([np.arange(T, dtype=f), np.full(NS, PAST, f)])
    ang = (pos[None, :] * inv[:, None]).astype(f)
    ang = np.concatenate([ang, ang], 0)
    for j in range(4):
        for s in range(9):
            c[32 * j + s, C_SUM + s] = 1.0
    c[:, C_ONE:C_ONE + 128] = 1.0
    hc = np.zeros((H_RT, 128, N_HC), f)
    for h in range(H_RT):
        lg = np.log1p(-(2.0 ** (-5.0 - h)))
        hc[h, :, HC_D:HC_D + 128] = np.where(i[None, :] >= i[:, None], np.exp(lg * np.maximum(i[None, :] - i[:, None], 0)), 0)
        hc[h, :, HC_IN:HC_IN + T] = np.exp(lg * (np.arange(T) % CH + 1.0))[None, :]
        hc[h, :, HC_ST] = np.exp(lg * (CH - 1.0 - i))
        hc[h, :, HC_CD:HC_CD + NC] = np.exp(lg * CH)
        hc[h, :, HC_G:HC_G + NS] = np.exp(lg)
    sel = np.zeros((H_ML, H_ML, HD), f)
    for h in range(H_ML):
        sel[h, h] = 1.0
    rp = np.concatenate([np.cos(ang), np.sin(ang)], 1).astype(f)
    return c, hc, rp, sel, lm


def program(nc, x_prompt, x_sample, st_hg, st_c, st_n, st_m, st_conv, st_rt, c_prompt, c_sample, g_norm,
            w_ada, b_ada, w_in, hgrn_lb, conv_w, conv_b, b_i, b_f, skip, w_gn, w_out, g_final,
            cst_d, hc_d, rope_d, sel_d, lm_d,
            y_p, y_s, hg_p, c_p, n_p, m_p, conv_p, rt_p, hg_s, c_s, n_s, m_s, conv_s, rt_s):
    with ExitStack() as ctx:
        def sb(name, *shape, dt=F32):
            return ctx.enter_context(nc.sbuf_tensor(name, list(shape), dt))

        def sem(name):
            return ctx.enter_context(nc.semaphore(name))

        pj = ctx.enter_context(nc.psum_tensor("pj", [P, 4, 512], F32))
        mx = ctx.enter_context(nc.psum_tensor("mx", [P, 4, 512], F32))
        cst = sb("cst", P, N_CST)
        lmask = sb("lmask", P, LEVELS * 128, dt=U8)
        with nc.sbuf_tensor("rows", [P, 2 * KB * TOK], F32) as rows_t:
            pass
        hh = sb("hh", P, KB, TOK, dt=F32R)
        hl = sb("hl", P, KB, TOK, dt=F32R)
        o = sb("o", P, KB, TOK)
        raw = sb("raw", P, RAW, KB * P // 2)
        whi = sb("whi", P, 2, KB * P, dt=F32R)
        wlo = sb("wlo", P, 2, KB * P, dt=F32R)
        x0, x1 = sb("x0", P, PAD + TOK), sb("x1", P, PAD + TOK)
        v, q, k = (sb(n, P, TOK) for n in ("v", "q", "k"))
        t1, t2, t3, t4 = (sb(n, P, TOK) for n in ("t1", "t2", "t3", "t4"))
        lev = sb("lev", P, LEVELS, T)
        qd, dt = sb("qd", P, T), sb("dt", P, T)
        z = x0[:, PAD:PAD + TOK]
        a = t1[:, 0:T].rearrange("p (c t) -> p c t", c=NC)
        kt = t2[:, 0:T].rearrange("p (c t) -> p c t", c=NC)
        vt = v[:, 0:NC * (HD + 1)].rearrange("p (c t) -> p c t", c=NC)
        ho = k[:, 0:T].rearrange("p (c t) -> p c t", c=NC)
        st = sb("st", P, NC, HD + 1)
        ss = sb("ss", P, NS, HD)
        ct = sb("ct", P, HD)
        big = lev[:, 4:6, :].rearrange("p a b -> p (a b)")
        r6 = lev[0:H_ML, LEVELS - 1, :]
        levf = lev[:].rearrange("p a b -> p (a b)")
        hc, rope_t = levf[:, 0:N_HC], levf[:, N_HC:N_HC + 2 * TOK]
        selh = sb("selh", H_ML, HD)
        cvr = sb("cvr", NS * PAD, 2, HD)
        cvc = sb("cvc", P, 2, NS * PAD)
        cvo = sb("cvo", PAD + NS, 2, HD)
        nr = sb("nr", NS, HD)
        sr = sb("sr", NS, 3, HD)
        sw = sb("sw", NS, HD)
        sm = sb("sm", P, 64)
        bst = sb("bst", P, NC + 1, 6)
        bag = sb("bag", P, NC + 1, 2)
        rstd = sb("rstd", P, NC + 1)
        prm = sb("prm", P, N_PRM)
        bia = sb("bia", P, N_BIAS)
        prow = sb("prow", P, P)
        brow = sb("brow", P, P)
        lbc = sb("lbc", P, 3, H_HG)
        sct = sb("sct", P, KB, 32)
        mod = sb("mod", P, 3 * KB, 9)
        ag = sb("ag", P, KB, 9)
        gw = sb("gw", P, KB, 2 * H_ML)
        gb = sb("gb", P, 2)
        iw6 = sb("iw6", H_ML, T)
        gcol = sb("gcol", P, H_ML, 4, NC)
        gs = sb("gs", NS, H_ML, 3)
        gsb = sb("gsb", P, H_ML, NS)
        g8 = sb("g8", H_ML, 12, NS)
        g4 = sb("g4", H_ML, 4, NC)
        m6 = sb("m6", H_ML, NS)

        hos = sw
        y_kept = nc.dram_tensor("y_kept", [DEPTH, P, KB * TOK], F32, kind="Internal").ap()

        def y_tile(n):
            return (t1, t2, t3, t4)[n % 4]

        ident = cst[:, C_ID:C_ID + 128]
        ones = cst[:, C_ONE:C_ONE + 128]
        ssum = cst[:, C_SUM:C_SUM + 9]

        spare = sem("spare")
        const_in, x_in, prm_in, gates_in = sem("const_in"), sem("x_in"), sem("prm_in"), sem("gates_in")
        ada_in = [sem(f"ada_in{j}") for j in range(RAW)]
        ada_used = sem("ada_used")
        raw_in = [sem(f"raw_in{j}") for j in range(2)]
        hi_done, lo_done = sem("hi_done"), sem("lo_done")
        tile_done = sem("tile_done")
        y_saved = sem("y_saved")
        y_in = [sem(f"y_in{j}") for j in range(4)]
        o_hi, o_lo = sem("o_hi"), sem("o_lo")
        xt_ready, xt_taken = sem("xt_ready"), sem("xt_taken")
        silu_c, sct_ready, sct_taken = sem("silu_c"), sem("sct_ready"), sem("sct_taken")
        init_done, c_exp, lb_diff, lb_ln = sem("init_done"), sem("c_exp"), sem("lb_diff"), sem("lb_ln")
        prm_tr, prm_taken = sem("prm_tr"), sem("prm_taken")
        ada_taken, ada_sum, mod_ready = sem("ada_taken"), sem("ada_sum"), sem("mod_ready")
        ms_ready, rs_made = sem("ms_ready"), sem("rs_made")
        sq_ready, sq_used, rs_ready = sem("sq_ready"), sem("sq_used"), sem("rs_ready")
        h_hi, hn_ready, h_ready, hs_ready = sem("h_hi"), sem("hn_ready"), sem("h_ready"), sem("hs_ready")
        taken = sem("taken")
        out_added = sem("out_added")
        head_done = sem("head_done")
        ps = {n: sem("p_" + n) for n in ("rot_q", "rot_k", "score", "tr", "u", "outer", "o", "os", "back", "cback",
                                         "conv", "bcast", "ostr")}
        vs = {n: sem("v_" + n) for n in ("qk", "a", "chain", "ss", "ho", "blk", "lev", "pred", "lf", "b",
                                         "conv_q", "conv_k", "r", "qd", "osc", "nrow", "kw", "d1", "var")}
        as_ = {n: sem("a_" + n) for n in ("vt", "kt", "sr", "l1", "l2", "kk", "eb", "lev", "cvc",
                                          "cvo", "dt", "silu", "z", "ct", "rs")}
        gsem = {n: sem("g_" + n) for n in ("proj", "a1", "v1", "a2", "tr", "col", "v2")}
        state_in, aux_in, stored = sem("state_in"), sem("aux_in"), sem("stored")
        fin_n, fin_t, fin_e, out_st = sem("fin_n"), sem("fin_t"), sem("fin_e"), sem("out_st")

        xrow = rows_t[:, 0:4 * D].rearrange("p (b d) -> p b d", b=4)
        crow, srow, e_row = (rows_t[0:n, (4 + m) * D:(5 + m) * D] for m, n in enumerate((9, NS, 9)))
        yrow, ysrow = xrow, srow

        def gi(l, base, i):
            return l * NH + base + i

        def auxc(l, kind, i):
            before = l * 16 * (4 * H_ML + H_RT + 1)
            return i * 64 + (before + 64) if kind == "ml" else i * 16 + (before + 64 * H_ML + 32)

        def scorec(l, kind, i, x):
            before = l * (H_HG * (LEVELS + 1) + H_ML + H_RT)
            if kind == "hg":
                return i * (LEVELS + 1) + (before + x)
            return i + (before + H_HG * (LEVELS + 1) + (H_ML if kind == "rt" else 0) + x)

        def held(e):
            e.sem_inc(spare, 1)

        def ht(g, j):
            return g * 4 + j + 3

        block = ctx.enter_context(nc.Block())
        GROUPS = ((H_HG, 0, "hg", COL_HG), (H_ML, H_HG, "ml", COL_ML), (H_RT, H_HG + H_ML, "rt", COL_RT))

        @block.sync
        def _(e):
            def load(t, par, src):
                e.wait_ge(lo_done, t - 1)
                held(e)
                for b in range(2):
                    e.dma_start(raw[:, 2 * par + b, :].rearrange("p (k n) -> p k n", k=KB // 2),
                                src[:, b * KB // 2:(b + 1) * KB // 2, :]).then_inc(raw_in[par], 16)

            e.dma_start(cst[:], cst_d).then_inc(const_in, 16)
            e.dma_start(levf[:, 0:LEVELS * 128], lm_d).then_inc(const_in, 16)
            e.dma_start(crow[0:1, :], c_prompt).then_inc(x_in, 16)
            e.dma_start(crow[1:9, :], c_sample).then_inc(x_in, 16)
            e.dma_start(srow, x_sample.rearrange("b t d -> (b t) d")).then_inc(x_in, 16)
            e.dma_start(xrow, x_prompt[0].rearrange("(b p) d -> p b d", p=P)).then_inc(x_in, 16)
            for l in range(DEPTH):
                wa = w_ada[l].rearrange("(k p) n -> p k n", p=P)
                wi = w_in[l].rearrange("(k p) n -> p k n", p=P)
                wo = w_out[l].rearrange("(k p) n -> p k n", p=P)
                if l:
                    e.wait_ge(prm_taken, 2 * l)
                    e.wait_ge(gsem["v2"], l)
                for r0, r1, src in (
                        (R_GN, R_SKIP, w_gn[l].rearrange("(r d) -> r d", d=HD)),
                        (R_SKIP, R_CW, skip[l].rearrange("(r d) -> r d", d=HD)),
                        (R_CW, R_CB, conv_w[l].rearrange("j (r d) -> (j r) d", d=HD)),
                        (R_CB, R_NORM, conv_b[l].rearrange("(r d) -> r d", d=HD)),
                        (R_NORM, R_LB, g_norm[l].rearrange("(r d) -> r d", d=HD)),
                        (R_LB, N_PRM, hgrn_lb.rearrange("l (r d) -> (l r) d", d=HD))):
                    e.dma_start(prow[r0:r1, :], src).then_inc(prm_in, 16)
                e.dma_start(brow[0:3 * KB, :], b_ada[l].rearrange("(r d) -> r d", d=HD)).then_inc(prm_in, 16)
                e.dma_start(brow[3 * KB:N_BIAS, :], g_final.rearrange("(r d) -> r d", d=HD)).then_inc(prm_in, 16)
                if l:
                    e.wait_ge(lo_done, l * TILES)
                for n in range(ADA_GROUPS):
                    for s in range(ADA_PIECES):
                        piece = (l * ADA_GROUPS + n) * ADA_PIECES + s
                        if piece >= RAW:
                            e.wait_ge(ada_used, piece - RAW + 1)
                        e.dma_start(raw[:, s % RAW, :].rearrange("p (k n) -> p k n", k=ADA_K),
                                    wa[:, ADA_K * s:ADA_K * (s + 1), n * ADA_N:(n + 1) * ADA_N]).then_inc(ada_in[s % RAW], 16)
                e.dma_start(gw[:], wi[:, :, COL_GATES:COL_GATES + 2 * H_ML]).then_inc(gates_in, 16)
                e.dma_start(gb[0:H_ML, 0:1], b_i[l].rearrange("(h a) -> h a", a=1)).then_inc(gates_in, 16)
                e.dma_start(gb[0:H_ML, 1:2], b_f[l].rearrange("(h a) -> h a", a=1)).then_inc(gates_in, 16)
                e.dma_start(m6[:], st_m[l].rearrange("b h -> h b"), allow_slow_non_contiguous=True).then_inc(gates_in, 16)
                if l == 0:
                    e.wait_ge(xt_taken, KB)
                    e.wait_ge(sct_taken, 2)
                e.dma_start(y_kept[l], o[:].rearrange("p k t -> p (k t)")).then_inc(y_saved, 16)
                e.dma_start(conv_s[l, :, 0:PAD - 1, :], st_conv[l, :, 1:PAD, :]).then_inc(stored, 16)
                e.wait_ge(ada_used, (l + 1) * ADA_GROUPS * ADA_PIECES)
                for j in range(2):
                    col = COL_HG[j]
                    if l:
                        e.wait_ge(lo_done, l * TILES)
                    for b in range(2):
                        e.dma_start(raw[:, 2 * j + b, :].rearrange("p (k n) -> p k n", k=KB // 2),
                                    wi[:, b * KB // 2:(b + 1) * KB // 2, col:col + HD]).then_inc(raw_in[j], 16)

                state = {"hg": (st_hg, hg_s), "ml": (st_c, c_s), "rt": (st_rt, rt_s)}
                n0 = l * STORES_PER_LAYER + 1
                for which, (count, base, kind, cols) in enumerate(GROUPS):
                    per = STORES[kind]
                    if kind == "rt":
                        e.dma_start(m_p[l].rearrange("b h -> h b"), g4[:, 3, NC - 1:NC],
                                    allow_slow_non_contiguous=True).then_inc(stored, 16)
                        e.dma_start(m_s[l].rearrange("b h -> h b"), g8[:, 3, :],
                                    allow_slow_non_contiguous=True).then_inc(stored, 16)
                        n0 += 2

                    def head(i, n0, nxt):
                        src, dst = state[kind]
                        g = i + (l * NH + base)
                        n = i + l * count
                        t = i * 4 + (l * TILES + 4 * base)
                        load(t + 2, 0, wi[:, :, bass.ds(i * HD + cols[2], HD)])
                        load(t + 3, 1, wi[:, :, bass.ds(i * HD + (COL_Z + base * HD), HD)])
                        e.wait_ge(stored, (i * per + n0) * 16)
                        held(e)
                        e.wait_ge(head_done, g + 1)
                        held(e)
                        e.dma_start(ss[:], src[l, :, bass.ds(i, 1)].rearrange("b h k v -> k (b h) v")).then_inc(state_in, 16)
                        if kind == "rt":
                            if isinstance(i, int) and i == 0:
                                e.dma_start(rope_t, rope_d).then_inc(aux_in, 16)
                            e.dma_start(hc, hc_d[bass.ds(i, 1)].rearrange("h p n -> (h p) n")).then_inc(aux_in, 16)
                        if kind == "ml":
                            e.dma_start(selh[:], sel_d[bass.ds(i, 1)].rearrange("h p n -> (h p) n")).then_inc(aux_in, 16)
                            for j in range(2):
                                e.dma_start(cvr[:, j, :], st_conv[l, :, :, bass.ds(i * HD + j * W_ML, HD)]
                                            .rearrange("b r d -> (b r) d")).then_inc(aux_in, 16)
                            e.dma_start(nr[:], st_n[l, :, bass.ds(i, 1)].rearrange("b h d -> (b h) d")).then_inc(aux_in, 16)
                        for j in range(2):
                            load(t + 4 + j, j, nxt(j))
                        if kind == "ml":
                            e.wait_ge(as_["cvo"], n + 1)
                            held(e)
                            for j in range(2):
                                cs = bass.ds(i * HD + j * W_ML, HD)
                                e.dma_start(conv_p[l, 0, :, cs], cvo[0:PAD, j, :]).then_inc(stored, 16)
                                e.dma_start(conv_s[l, :, PAD - 1, cs], cvo[PAD:PAD + NS, j, :]).then_inc(stored, 16)
                        e.wait_ge(vs["ss"], g + 1)
                        held(e)
                        e.dma_start(dst[l, :, bass.ds(i, 1)].rearrange("b h k v -> k (b h) v"), ss[:]).then_inc(stored, 16)
                        if kind == "ml":
                            e.wait_ge(vs["nrow"], n + 1)
                            held(e)
                            e.dma_start(n_s[l, :, bass.ds(i, 1)].rearrange("b h d -> (b h) d"), nr[:]).then_inc(stored, 16)
                            e.dma_start(n_p[l, 0, bass.ds(i, 1)].rearrange("h d -> d h"), st[:, NC - 1, HD:HD + 1],
                                        allow_slow_non_contiguous=True).then_inc(stored, 16)
                            e.wait_ge(as_["ct"], n + 1)
                            held(e)
                            e.dma_start(c_p[l, 0, bass.ds(i, 1)].rearrange("h v k -> (h v) k"), ct[:]).then_inc(stored, 16)
                        else:
                            e.wait_ge(vs["chain"], g + 1)
                            held(e)
                            out = hg_p if kind == "hg" else rt_p
                            e.dma_start(out[l, 0, bass.ds(i, 1)].rearrange("h k v -> (h k) v"),
                                        st[:, NC - 1, 0:HD]).then_inc(stored, 16)

                    first = 0
                    if kind == "rt":
                        head(0, n0, lambda j: wi[:, :, cols[j] + HD:cols[j] + 2 * HD])
                        first = 1
                    with e.Fori(first, count - 1) as i:
                        head(i, n0, lambda j: wi[:, :, bass.ds(i * HD + (cols[j] + HD), HD)])
                    if which + 1 < len(GROUPS):
                        after = GROUPS[which + 1][3]
                        head(count - 1, n0, lambda j: wi[:, :, after[j]:after[j] + HD])
                    else:
                        head(count - 1, n0, lambda j: wo[:, :, j * P:(j + 1) * P])
                    n0 += per * count
                t = l * TILES + 4 * NH
                e.wait_ge(head_done, (l + 1) * NH + 1)
                e.wait_ge(y_saved, (l + 1) * 16)

                def y_load(n):
                    if n >= 4:
                        e.wait_ge(out_added, l * KB + n - 3)
                    e.dma_start(y_tile(n)[:], y_kept[l, :, n * TOK:(n + 1) * TOK]).then_inc(y_in[n % 4], 16)

                for n in range(3):
                    y_load(n)
                for n in range(2, KB):
                    load(t + n, n % 2, wo[:, :, n * P:(n + 1) * P])
                    if n + 1 < KB:
                        y_load(n + 1)
            e.wait_ge(fin_e, KB + 4)
            e.dma_start(y_p[0].rearrange("(b p) d -> p b d", p=P), yrow).then_inc(out_st, 16)
            e.dma_start(y_s.rearrange("b t d -> (b t) d"), ysrow).then_inc(out_st, 16)
            e.wait_ge(out_st, 32)
            e.wait_ge(stored, DEPTH * STORES_PER_LAYER * 16)

        @block.gpsimd
        def _(e):
            def low(t, par):
                e.wait_ge(hi_done, t + 1)
                e.tensor_tensor(wlo[:, par, :], raw[:, 2 * par:2 * par + 2, :].rearrange("p a b -> p (a b)"),
                                whi[:, par, :].bitcast(F32), ALU.subtract).then_inc(lo_done, 1)

            def low_o(l, kb):
                e.wait_ge(o_hi, l * KB + kb + 1)
                e.tensor_tensor(hl[:, kb, :], o[:, kb, :], hh[:, kb, :].bitcast(F32), ALU.subtract).then_inc(o_lo, 1)

            for l in range(DEPTH):
                for j in range(2):
                    low(l * TILES + j, j)
                with e.Fori(0, NH) as i:
                    for j in range(2, 6):
                        low(i * 4 + (l * TILES + j), j % 2)
                for kb in range(KB):
                    low_o(l, kb)
                for n in range(2, KB):
                    low(l * TILES + 4 * NH + n, n % 2)

        @block.tensor
        def _(e):
            def quarter(par, part, ready=None, l=0):
                for kb in range(4 * part, 4 * part + 4):
                    if ready is not None:
                        e.wait_ge(ready, l * KB + kb + 1)
                    for m, (w, x) in enumerate(((whi, hh), (whi, hl), (wlo, hh))):
                        for b in range(2):
                            last = e.matmul(pj[:, 2 * par + b, 0:HALF], w[:, par, kb * P:(kb + 1) * P],
                                            x[:, kb, b * HALF:(b + 1) * HALF],
                                            start=(kb == 0 and m == 0), stop=(kb == KB - 1 and m == 2))
                return last

            def tr(out, src, n):
                return e.transpose(out, src, cst[0:n, C_ID:C_ID + n])

            e.wait_ge(const_in, 32)
            e.wait_ge(silu_c, 1)
            for kb in range(KB):
                last = tr(mx[:, 2, kb * 9:kb * 9 + 9], crow[:, kb * P:(kb + 1) * P], 9)
            last.then_inc(sct_ready, 1)
            e.wait_ge(x_in, 64)
            for kb in range(KB):
                last = tr(mx[:, 3, kb * NS:(kb + 1) * NS], srow[:, kb * P:(kb + 1) * P], NS)
            last.then_inc(sct_ready, 1)
            for kb in range(KB):
                if kb >= 4:
                    e.wait_ge(xt_taken, kb - 3)
                for b in range(4):
                    last = tr(pj[:, kb % 4, b * P:(b + 1) * P], xrow[:, b, kb * P:(kb + 1) * P], P)
                last.then_inc(xt_ready, 1)
            e.wait_ge(xt_taken, KB)
            e.wait_ge(sct_taken, 2)

            def norm(n):
                for kb in range(KB):
                    e.wait_ge(sq_ready, n * KB + kb + 1)
                    for b in range(2):
                        last = e.matmul(mx[:, b, 0:HALF], ones, (t1, t2)[kb % 2][:, b * HALF:(b + 1) * HALF],
                                        start=(kb == 0), stop=(kb == KB - 1))
                    last.then_inc(sq_used, 1)

            for l in range(DEPTH):
                t0 = l * TILES
                if l:
                    e.wait_ge(out_added, l * KB)
                e.wait_ge(prm_in, (l + 1) * 128)
                tr(mx[:, 1, 0:N_PRM], prow[0:N_PRM, :], N_PRM)
                tr(mx[:, 1, 128:128 + N_BIAS], brow[0:N_BIAS, :], N_BIAS).then_inc(prm_tr, 1)

                def ada_columns(n):
                    e.wait_ge(ada_taken, l * ADA_GROUPS + n + 1)
                    for c in range(4):
                        last = e.matmul(mx[:, 0, (4 * n + c) * 9:(4 * n + c) * 9 + 9],
                                        (t1, t2)[n % 2][:, c * P:(c + 1) * P], ssum, start=True, stop=True)
                    last.then_inc(ada_sum, 1)

                for n in range(ADA_GROUPS):
                    if n >= 2:
                        e.wait_ge(ada_taken, l * ADA_GROUPS + n - 1)
                    for s in range(ADA_PIECES):
                        piece = (l * ADA_GROUPS + n) * ADA_PIECES + s
                        e.wait_ge(ada_in[s % RAW], 16 * (piece // RAW + 1))
                        for j in range(ADA_K):
                            kb = ADA_K * s + j
                            r = 32 * (kb % 4)
                            last = e.matmul(pj[r:r + 32, n % 2, :], sct[:, kb, :],
                                            raw[:, s % RAW, j * ADA_N:(j + 1) * ADA_N], start=(kb < 4), stop=(kb >= KB - 4))
                        last.then_inc(ada_used, 1)
                    if n:
                        ada_columns(n - 1)
                ada_columns(ADA_GROUPS - 1)
                e.wait_ge(mod_ready, l + 1)
                norm(l)

                def tile_wait(t, j, g):
                    e.wait_ge(lo_done, t + 1)
                    e.wait_ge(taken, g * 4 + (j + 1))

                def whole(t, j, g, between=()):
                    tile_wait(t + j, j, g)
                    for part in range(4):
                        last = quarter(j % 2, part)
                        if part == 3:
                            last.then_inc(tile_done, 1)
                        if part < len(between) and between[part]:
                            between[part]()

                e.wait_ge(hs_ready, l + 1)
                tile_wait(t0, 0, l * NH)
                for part in range(4):
                    last = quarter(0, part, h_ready, l)
                last.then_inc(tile_done, 1)
                for count, base, kind, _cols in GROUPS:
                    if kind == "ml":
                        e.wait_ge(gates_in, (l + 1) * 64)
                        e.wait_ge(head_done, l * NH + H_HG + 1)
                        for kb in range(KB):
                            for m, x in enumerate((hh, hl)):
                                for j in range(4):
                                    w = gw[:, kb, (j % 2) * H_ML:(j % 2 + 1) * H_ML]
                                    last = e.matmul(mx[32 * j:32 * j + H_ML, 0, 0:HALF], w,
                                                    x[:, kb, (j // 2) * HALF:(j // 2 + 1) * HALF].bitcast(F32),
                                                    start=(kb == 0 and m == 0), stop=(kb == KB - 1 and m == 1))
                        last.then_inc(gsem["proj"], 1)
                        e.wait_ge(gsem["v2"], l + 1)
                        for what in range(3):
                            for c in range(NC):
                                tr(mx[:, 1, (what * NC + c) * 8:(what * NC + c) * 8 + H_ML],
                                   lev[0:H_ML, 2 + what, c * CH:(c + 1) * CH], H_ML)
                        for what in range(3):
                            tr(mx[0:NS, 2, what * 8:what * 8 + H_ML], g8[:, what, :], H_ML)
                        e.matmul(mx[:, 3, 0:H_ML * NC], cst[0:H_ML, C_ONE:C_ONE + 128], lev[0:H_ML, 5, 0:H_ML * NC],
                                 start=True, stop=True)
                        e.matmul(mx[:, 3, 64:64 + H_ML * NS], cst[0:H_ML, C_ONE:C_ONE + 128],
                                 lev[0:H_ML, 5, 64:64 + H_ML * NS], start=True, stop=True).then_inc(gsem["tr"], 1)
                        e.wait_ge(gsem["col"], l + 1)

                    def head(i, last_head):
                        g = i + (l * NH + base)
                        n = i + l * count
                        t = i * 4 + (t0 + 4 * base)

                        def sample_rows():
                            e.wait_ge(vs["qk"], g + 1)
                            for j, src in enumerate((x1 if kind == "hg" else q, k, v)):
                                s0 = PAD + T if (kind == "hg" and j == 0) else T
                                last = tr(mx[0:NS, 3, j * HD:(j + 1) * HD], src[:, s0:s0 + NS], P)
                            return last

                        def v_rows():
                            e.wait_ge(taken, ht(g, 2))
                            for c in range(NC):
                                tr(mx[:, 1, c * HD:(c + 1) * HD], v[:, c * CH:(c + 1) * CH], P)

                        def k_rows():
                            kw = dt if kind == "hg" else k
                            for c in range(NC):
                                tr(mx[:, 2, c * HD:(c + 1) * HD], kw[:, c * CH:(c + 1) * CH], P)

                        def rows():
                            if kind == "hg":
                                e.wait_ge(vs["kw"], n + 1)
                                e.wait_ge(vs["a"], g + 1)
                            else:
                                e.wait_ge(vs["qk"], g + 1)
                            v_rows()
                            k_rows()
                            sample_rows().then_inc(ps["tr"], 1)

                        def scores():
                            e.wait_ge(vs["qk"], g + 1)
                            if kind == "ml":
                                e.wait_ge(as_["cvc"], n + 1)
                                e.wait_ge(as_["cvo"], n + 1)
                                e.wait_ge(as_["dt"], n + 1)
                                e.wait_ge(vs["qd"], n + 1)
                            for c in range(NC):
                                last = e.matmul(mx[:, 0, c * CH:(c + 1) * CH], k[:, c * CH:(c + 1) * CH],
                                                q[:, c * CH:(c + 1) * CH], start=True, stop=True)
                            last.then_inc(ps["score"], 1)

                        def rot(j):
                            def run():
                                e.wait_ge(taken, ht(g, j))
                                src = (x0, x1)[j]
                                for b in range(2):
                                    last = e.matmul(mx[:, 2 * j + b, 0:HALF], cst[:, C_ROT:C_ROT + 128],
                                                    src[:, PAD + b * HALF:PAD + (b + 1) * HALF], start=True, stop=True)
                                last.then_inc(ps[("rot_q", "rot_k")[j]], 1)
                            return run

                        def level_scores(vs_range):
                            def run():
                                for lv in vs_range:
                                    if lv < 0:
                                        e.wait_ge(vs["qk"], g + 1)
                                    else:
                                        e.wait_ge(vs["lev"], n * LEVELS + (lv + 1))
                                    if lv >= 3:
                                        e.wait_ge(vs["pred"], n * (LEVELS + 1) + (lv - 2))
                                    bank = (lv + 1) % 4
                                    for c in range(NC):
                                        cs = slice(c * CH, (c + 1) * CH)
                                        if lv < 0:
                                            last = e.matmul(mx[:, bank, cs], k[:, cs], x1[:, PAD + c * CH:PAD + (c + 1) * CH],
                                                            start=True, stop=True)
                                        else:
                                            last = e.matmul(mx[:, bank, cs], lev[:, lv, cs], lev[:, lv, cs],
                                                            start=True, stop=True)
                                    last.then_inc(ps["score"], 1)
                            return run

                        def states_u():
                            e.wait_ge(vs["a"], g + 1)
                            e.wait_ge(vs["blk"], g + 1)
                            e.wait_ge(as_["vt"], g + 1)
                            e.wait_ge(as_["kt"], g + 1)
                            e.wait_ge(as_["sr"], g + 1)
                            w = HD + 1 if kind == "ml" else HD
                            for c in range(NC):
                                last = e.matmul(mx[:, c // 2, (c % 2) * 129:(c % 2) * 129 + w], kt[:, c, :], vt[:, c, 0:w],
                                                start=True, stop=True)
                            last.then_inc(ps["u"], 1)
                            lhs = sw[:] if kind == "ml" else sr[:, 1, :]
                            for b in range(2):
                                last = e.matmul(mx[:, 2 + b, :], lhs, big[0:NS, b * 512:(b + 1) * 512], start=True, stop=True)
                            last.then_inc(ps["outer"], 1)

                        def outputs():
                            e.wait_ge(vs["chain"], g + 1)
                            w = HD + 1 if kind == "ml" else HD
                            for c in range(NC):
                                out = mx[:, c // 2, (c % 2) * 129:(c % 2) * 129 + w]
                                last = e.matmul(out, a[:, c, :], vt[:, c, 0:w], start=True, stop=(c == 0))
                                if c:
                                    last = e.matmul(out, qd[:, c * CH:(c + 1) * CH], st[:, c - 1, 0:w], start=False, stop=True)
                            last.then_inc(ps["o"], 1)
                            e.wait_ge(vs["ss"], g + 1)
                            if kind == "ml":
                                for b in range(2):
                                    last = e.matmul(mx[:, 2 + b, :], cst[0:NS, C_ONE:C_ONE + 128],
                                                    lev[0:NS, b, :], start=True, stop=True)
                            else:
                                qs = x1[:, PAD + T:PAD + TOK] if kind == "hg" else q[:, T:TOK]
                                for b in range(2):
                                    last = e.matmul(mx[0:NS, 2 + b, :], qs,
                                                    ss[:, 4 * b:4 * b + 4, :].rearrange("p s v -> p (s v)"),
                                                    start=True, stop=True)
                            last.then_inc(ps["os"], 1)

                        def ml_os():
                            e.wait_ge(vs["osc"], n + 1)
                            tr(mx[0:NS, 2, 0:HD], sm[:, 40:48], P).then_inc(ps["ostr"], 1)
                            tr(mx[:, 3, 128:256], st[:, NC - 1, 0:HD], P).then_inc(ps["cback"], 1)

                        def back():
                            if kind == "ml":
                                e.wait_ge(as_["ct"], n + 1)
                            e.wait_ge(vs["ho"], g + 1)
                            for c in range(NC):
                                tr(mx[:, 2, c * CH:(c + 1) * CH], ho[:, c, :], P)
                            tr(mx[:, 3, 0:NS], hos[:], NS).then_inc(ps["back"], 1)

                        def ml_first():
                            e.wait_ge(head_done, g + 1)
                            e.wait_ge(aux_in, auxc(l, kind, i))
                            e.matmul(mx[:, 0, :], selh[:], r6, start=True, stop=True)
                            e.matmul(mx[:, 1, :], selh[:], iw6[:], start=True, stop=True)
                            for j in range(2):
                                last = tr(mx[:, 3, 24 * j:24 * j + 24], cvr[:, j, :], NS * PAD)
                            last.then_inc(ps["bcast"], 1)

                        def ml_conv():
                            e.wait_ge(taken, ht(g, 1))
                            for j, src in enumerate((x0, x1)):
                                last = tr(mx[0:PAD + NS, 2, j * HD:(j + 1) * HD], src[:, T:T + PAD + NS], P)
                            last.then_inc(ps["conv"], 1)

                        if kind == "rt":
                            whole(t, 1, g)
                            whole(t, 2, g, (rot(0), None, rot(1)))
                            whole(t, 3, g, (lambda: (scores(), rows()), None, states_u, outputs))
                        elif kind == "ml":
                            whole(t, 1, g, (None, ml_first))
                            whole(t, 2, g, (ml_conv,))
                            whole(t, 3, g, (lambda: (scores(), rows()), None, states_u, outputs))
                        else:
                            whole(t, 1, g)
                            whole(t, 2, g, (None, None, None, level_scores((-1, 0, 1, 2))))
                            whole(t, 3, g, (level_scores((3, 4, 5, 6)), rows, states_u, outputs))
                        if last_head:
                            e.wait_ge(lo_done, t + 5)
                            e.wait_ge(taken, g * 4 + 5)
                        else:
                            tile_wait(t + 4, 0, g + 1)
                        for part in range(3 if last_head else 4):
                            last = quarter(0, part, o_lo if last_head else None, l)
                            if part == 3:
                                last.then_inc(tile_done, 1)
                            if part == 0 and kind == "ml":
                                ml_os()
                        back()

                    if kind == "rt":
                        with e.Fori(0, count - 1) as i:
                            head(i, False)
                        head(count - 1, True)
                    else:
                        with e.Fori(0, count) as i:
                            head(i, False)

                e.wait_ge(head_done, (l + 1) * NH + 1)
                for n in range(KB):
                    e.wait_ge(lo_done, t0 + 4 * NH + n + 1)
                    if n >= 2:
                        e.wait_ge(out_added, l * KB + n - 1)
                    else:
                        e.wait_ge(taken, (l + 1) * NH * 4 + 2)
                    for part in range(0 if n else 3, 4):
                        last = quarter(n % 2, part, None if n else o_lo, l)
                    last.then_inc(tile_done, 1)
            e.wait_ge(out_added, DEPTH * KB)
            norm(DEPTH)
            for b in range(4):
                for m in range(4):
                    i = 4 * b + m
                    e.wait_ge(fin_n, 4 * m + 4 if b == 0 else KB)
                    if i >= 4:
                        e.wait_ge(fin_e, i - 3)
                    for c in range(4):
                        last = tr(pj[:, i % 4, c * P:(c + 1) * P], o[:, 4 * m + c, b * P:(b + 1) * P], P)
                    last.then_inc(fin_t, 1)
            e.wait_ge(rs_ready, 1)
            for kb in range(KB):
                last = tr(mx[0:NS, kb // 4, (kb % 4) * P:(kb % 4 + 1) * P], o[:, kb, T:TOK], P)
            last.then_inc(fin_t, 1)

        @block.scalar
        def _(e):
            def act(out, in_, func, **kw):
                return e.activation(out, in_, func, **kw)

            e.wait_ge(x_in, 64)
            act(e_row, crow, ACT.Exp, scale=-1.0).then_inc(c_exp, 1)
            e.drain().then_inc(taken, 2)
            e.wait_ge(sct_ready, 1)
            e.wait_ge(init_done, 1)
            act(sct[:, :, 0:9], mx[:, 2, 0:9 * KB].rearrange("p (k s) -> p k s", s=9), ACT.Copy).then_inc(sct_taken, 1)
            e.wait_ge(sct_ready, 2)
            act(o[:, :, T:TOK], mx[:, 3, 0:NS * KB].rearrange("p (k s) -> p k s", s=NS), ACT.Copy).then_inc(sct_taken, 1)
            for kb in range(KB):
                e.wait_ge(xt_ready, kb + 1)
                act(o[:, kb, 0:T], pj[:, kb % 4, :], ACT.Copy).then_inc(xt_taken, 1)

            def high(t, half, par, used=True):
                e.wait_ge(raw_in[par], half * 32)
                if used:
                    e.wait_ge(tile_done, t - 1)
                act(whi[:, par, :], raw[:, 2 * par:2 * par + 2, :].rearrange("p a b -> p (a b)"), ACT.Copy).then_inc(hi_done, 1)

            def high_o(l, kb):
                act(hh[:, kb, :], o[:, kb, :], ACT.Copy).then_inc(o_hi, 1)

            def norm(n):
                for kb in range(KB):
                    if n * KB + kb >= 2:
                        e.wait_ge(sq_used, n * KB + kb - 1)
                    act((t1, t2)[kb % 2][:], o[:, kb, :], ACT.Square).then_inc(sq_ready, 1)
                e.wait_ge(ms_ready, n + 1)
                act(t3[:], t3[:], ACT.Ln)
                e.drain()
                act(t3[:], t3[:], ACT.Exp, scale=-0.5).then_inc(rs_made, 1)

            for l in range(DEPTH):
                e.wait_ge(prm_tr, l + 1)
                act(prm[:], mx[:, 1, 0:N_PRM], ACT.Copy).then_inc(prm_taken, 1)
                act(bia[:], mx[:, 1, 128:128 + N_BIAS], ACT.Copy).then_inc(prm_taken, 1)
                for n in range(ADA_GROUPS):
                    e.wait_ge(ada_used, (l * ADA_GROUPS + n + 1) * ADA_PIECES)
                    if n >= 2:
                        e.wait_ge(ada_sum, l * ADA_GROUPS + n - 1)
                    act((t1, t2)[n % 2][:, 0:512], pj[:, n % 2, :], ACT.Copy).then_inc(ada_taken, 1)
                e.wait_ge(mod_ready, l + 1)
                if l:
                    e.wait_ge(lb_diff, 1)
                    act(lbc[:, 2, :], lbc[:, 2, :], ACT.Exp, scale=-1.0)
                    e.drain()
                    act(lbc[:, 2, :], lbc[:, 2, :], ACT.Ln, bias=1.0).then_inc(lb_ln, 1)
                norm(l)
                for j in range(2):
                    high(l * TILES + j, l * TILES // 2 + 1, j, l > 0)
                for kb in range(KB):
                    e.wait_ge(hn_ready, l * KB + kb + 1)
                    act(hh[:, kb, 0:T], (t1, t2)[kb % 2][:, 0:T], ACT.Identity, bias=mod[:, kb, 0:1]).then_inc(h_hi, 1)

                for count, base, kind, _cols in GROUPS:
                    if kind == "ml":
                        e.wait_ge(gsem["proj"], l + 1)
                        for b in range(2):
                            act(t1[0:H_ML, b * HALF:(b + 1) * HALF],
                                mx[64 * b:64 * b + H_ML, 0, 0:HALF], ACT.Identity, bias=gb[0:H_ML, 0:1])
                            act(t2[0:H_ML, b * HALF:(b + 1) * HALF],
                                mx[64 * b + 32:64 * b + 32 + H_ML, 0, 0:HALF], ACT.Identity, bias=gb[0:H_ML, 1:2])
                        e.drain()
                        act(t3[0:H_ML, :], t2[0:H_ML, :], ACT.Abs)
                        e.drain()
                        act(t3[0:H_ML, :], t3[0:H_ML, :], ACT.Exp, scale=-1.0)
                        e.drain()
                        act(t3[0:H_ML, :], t3[0:H_ML, :], ACT.Ln, bias=1.0).then_inc(gsem["a1"], 1)
                        e.wait_ge(gsem["v1"], l + 1)
                        act(iw6[:], iw6[:], ACT.Exp)
                        act(lev[0:H_ML, 3, :], lev[0:H_ML, 3, :], ACT.Exp)
                        act(lev[0:H_ML, 4, :], lev[0:H_ML, 4, :], ACT.Exp, scale=-1.0)
                        act(g4[:, 2, :], g4[:, 2, :], ACT.Exp)
                        act(g8[:, 0:2, :], g8[:, 4:6, :], ACT.Exp)
                        act(g8[:, 2, :], g8[:, 3, :], ACT.Exp, scale=-1.0).then_inc(gsem["a2"], 1)

                    def head(i, last_head):
                        g = i + (l * NH + base)
                        n = i + l * count

                        def take(j, dst, off, scale=1.0):
                            t = i * 4 + (l * TILES + 4 * base + j)
                            e.wait_ge(tile_done, t + 1)
                            for b in range(2):
                                last = act(dst[:, off + b * HALF:off + (b + 1) * HALF], pj[:, 2 * (j % 2) + b, 0:HALF],
                                           ACT.Copy, scale=scale)
                            last.then_inc(taken, 1)
                            high(t + 2, i * 2 + ((l * TILES + 4 * base + j + 2) // 2 + 1), j % 2)

                        def rows(scaled):
                            e.wait_ge(ps["tr"], g + 1)
                            act(vt[:, :, 0:HD], mx[:, 1, :].rearrange("p (c d) -> p c d", c=NC), ACT.Copy).then_inc(as_["vt"], 1)
                            if scaled == "ml":
                                e.wait_ge(vs["r"], n + 1)
                                for c in range(NC):
                                    last = act(kt[:, c, :], mx[:, 2, c * HD:(c + 1) * HD], ACT.Copy, scale=sm[:, 4 + c:5 + c])
                            else:
                                last = act(kt, mx[:, 2, :].rearrange("p (c d) -> p c d", c=NC), ACT.Copy,
                                           scale=hc[:, HC_ST:HC_ST + 1] if scaled == "rt" else 1.0)
                            last.then_inc(as_["kt"], 1)
                            act(sr[:], mx[0:NS, 3, 0:3 * HD].rearrange("p (j d) -> p j d", j=3), ACT.Copy).then_inc(as_["sr"], 1)

                        def z_exp():
                            act(t4[:], z, ACT.Exp, scale=-1.0).then_inc(as_["z"], 1)

                        e.wait_ge(head_done, g + 1)
                        if kind == "rt":
                            take(0, x0, PAD)
                            take(1, x1, PAD, SCALE)
                            take(2, v, 0)
                            e.wait_ge(aux_in, auxc(l, kind, i))
                            rows("rt")
                        elif kind == "ml":
                            take(0, x0, PAD)
                            e.wait_ge(ps["bcast"], n + 1)
                            act(cvc[:], mx[:, 3, 0:48].rearrange("p (j r) -> p j r", j=2), ACT.Copy).then_inc(as_["cvc"], 1)
                            e.wait_ge(vs["r"], n + 1)
                            act(dt[:], dt[:], ACT.Exp).then_inc(as_["dt"], 1)
                            e.wait_ge(vs["conv_q"], n + 1)
                            act(t3[:], t1[:], ACT.Exp, scale=-1.0).then_inc(as_["silu"], 1)
                            take(1, x1, PAD)
                            e.wait_ge(ps["conv"], n + 1)
                            act(cvo[:], mx[0:PAD + NS, 2, 0:2 * HD].rearrange("p (j d) -> p j d", j=2), ACT.Copy).then_inc(as_["cvo"], 1)
                            e.wait_ge(vs["conv_k"], n + 1)
                            act(t4[:], t2[:], ACT.Exp, scale=-1.0).then_inc(as_["silu"], 1)
                            take(2, v, 0)
                            rows("ml")
                        else:
                            take(0, x0, PAD)
                            f = x0[:, PAD:PAD + TOK]
                            e.drain()
                            act(t1[:], f, ACT.Abs)
                            e.drain()
                            act(t1[:], t1[:], ACT.Exp, scale=-1.0)
                            e.drain()
                            act(t1[:], t1[:], ACT.Ln, bias=1.0).then_inc(as_["l1"], 1)
                            e.wait_ge(vs["d1"], n + 1)
                            act(k[:], t4[:], ACT.Exp, bias=sm[:, 9:10]).then_inc(as_["kk"], 1)
                            act(t3[:], t3[:], ACT.Exp, scale=-1.0)
                            e.drain()
                            act(t3[:], t3[:], ACT.Ln, bias=1.0).then_inc(as_["l2"], 1)
                            take(1, x1, PAD, SCALE)
                            e.wait_ge(vs["b"], n + 1)
                            act(qd[:], t2[:, 0:T], ACT.Exp)
                            act(sm[:, 16:20], t2[:, CH - 1:T:CH], ACT.Exp)
                            act(sm[:, 24:32], t3[:, T:TOK], ACT.Exp)
                            act(dt[:], t4[:, 0:T], ACT.Exp, scale=-1.0).then_inc(as_["eb"], 1)
                            for lv in range(LEVELS):
                                e.wait_ge(vs["lf"], n * LEVELS + (lv + 1))
                                x = 64 >> lv
                                w = lev[:, lv, :].rearrange("p (n s x) -> p n s x", s=2, x=x)
                                act(w[:, :, 0, :], w[:, :, 0, :], ACT.Exp, scale=-1.0)
                                act(w[:, :, 1, :], w[:, :, 1, :], ACT.Exp).then_inc(as_["lev"], 1)
                            take(2, v, 0)
                            rows("hg")
                        e.wait_ge(vs["a"], g + 1)
                        take(3, x0, PAD)
                        e.drain()
                        z_exp()
                        if last_head:
                            for kb in range(KB - 1):
                                high_o(l, kb)
                        if kind == "ml":
                            e.wait_ge(ps["cback"], n + 1)
                            act(ct[:], mx[:, 3, 128:256], ACT.Copy).then_inc(as_["ct"], 1)
                        e.wait_ge(vs["var"], g + 1)
                        act(rstd[:], bag[:, :, 1], ACT.Ln)
                        e.drain()
                        act(rstd[:], rstd[:], ACT.Exp, scale=-0.5).then_inc(as_["rs"], 1)

                    if kind == "rt":
                        with e.Fori(0, count - 1) as i:
                            head(i, False)
                        head(count - 1, True)
                    else:
                        with e.Fori(0, count) as i:
                            head(i, False)
                e.wait_ge(head_done, (l + 1) * NH + 1)
                high_o(l, KB - 1)
                for n in range(2, KB):
                    t = l * TILES + 4 * NH + n
                    high(t, t // 2 + 1, n % 2)
            e.wait_ge(out_added, DEPTH * KB)
            norm(DEPTH)
            for i in range(16):
                e.wait_ge(fin_t, i + 1)
                act(yrow[:, i // 4, (i % 4) * 512:(i % 4 + 1) * 512], pj[:, i % 4, :], ACT.Copy).then_inc(fin_e, 1)
            e.wait_ge(fin_t, 17)
            for b in range(4):
                act(ysrow[:, b * 512:(b + 1) * 512], mx[0:NS, b, :], ACT.Copy).then_inc(fin_e, 1)

        @block.vector
        def _(e):
            def tt(out, a_, b_, op):
                return e.tensor_tensor(out, a_, b_, op)

            def ts(out, a_, s1, s2, op0, op1=None):
                return e.tensor_scalar(out, a_, s1, s2, op0, op1) if op1 is not None else e.tensor_scalar(out, a_, s1, None, op0)

            def stt(out, a_, s, b_, op0, op1):
                return e.scalar_tensor_tensor(out=out, in0=a_, scalar=s, in1=b_, op0=op0, op1=op1)

            def bc(ap, axis, n):
                return ap.unsqueeze(axis).broadcast_to([*ap.shape[:axis], n, *ap.shape[axis:]])

            def absolute(out, a_):
                return stt(out, a_, -1.0, a_, ALU.mult, ALU.max)

            def chunk_sums(out, a_, r):
                for c in range(NC):
                    cs = slice(c * CH, (c + 1) * CH)
                    e.tensor_tensor_scan(out[:, cs], ones[r, :], a_[:, cs], 0.0, ALU.mult, ALU.add)

            M, A_, S_, MAX, MIN = ALU.mult, ALU.add, ALU.subtract, ALU.max, ALU.min

            e.memset(sct[:], 0.0)
            e.memset(x0[:, 0:PAD], 0.0)
            e.memset(x1[:, 0:PAD], 0.0)
            e.memset(g4[:], 0.0)
            e.memset(bag[:], 1.0)
            e.drain().then_inc(init_done, 1)
            e.sem_inc(head_done, 1)
            e.wait_ge(c_exp, 1)
            ts(e_row, e_row, 1.0, None, A_)
            e.drain()
            e.reciprocal(e_row, e_row)
            e.drain()
            tt(crow, crow, e_row, M).then_inc(silu_c, 1)
            e.wait_ge(const_in, 32)
            ts(lmask[:], levf[:, 0:LEVELS * 128], 0.5, None, ALU.is_gt)

            def norm(n, last=False):
                e.wait_ge(sq_used, (n + 1) * KB)
                for b in range(2):
                    ts(t3[:, b * HALF:(b + 1) * HALF], mx[:, b, 0:HALF], 1.0 / D, EPS, M, A_)
                e.drain().then_inc(ms_ready, 1)
                e.wait_ge(rs_made, n + 1)

            for l in range(DEPTH):
                e.wait_ge(ada_sum, (l + 1) * ADA_GROUPS)
                e.wait_ge(prm_taken, 2 * (l + 1))
                tt(mod[:], mx[:, 0, 0:27 * KB].rearrange("p (k s) -> p k s", s=9), bc(bia[:, 0:3 * KB], 2, 9), A_)
                e.drain()
                stt(ag[:], mod[:, KB:2 * KB, :], 1.0, bc(prm[:, R_NORM:R_NORM + KB], 2, 9), A_, M).then_inc(mod_ready, 1)
                lb0, lb1 = prm[:, R_LB:R_LB + H_HG], prm[:, R_LB + H_HG:R_LB + 2 * H_HG]
                if l == 0:
                    e.memset(lbc[:, 0, :], -1e30)
                    e.memset(lbc[:, 1, :], 0.0)
                else:
                    tt(lbc[:, 2, :], lb0, lb1, S_)
                    tt(sm[:, 0:4], lb0, lb1, MAX)
                    e.drain()
                    absolute(lbc[:, 2, :], lbc[:, 2, :])
                    tt(sm[:, 4:8], lb1, sm[:, 0:4], S_)
                    tt(sm[:, 8:12], lb0, sm[:, 0:4], S_)
                    e.drain().then_inc(lb_diff, 1)
                    e.wait_ge(lb_ln, 1)
                    tt(lbc[:, 0, :], sm[:, 4:8], lbc[:, 2, :], S_)
                    tt(lbc[:, 1, :], sm[:, 8:12], lbc[:, 2, :], S_)
                norm(l)
                hs = t4[:, 0:KB * NS].rearrange("p (k s) -> p k s", s=NS)
                tt(hs, o[:, :, T:TOK], bc(t3[:, T:TOK], 1, KB), M)
                e.drain()
                tt(hs, hs, ag[:, :, 1:9], M)
                e.drain()
                tt(hs, hs, mod[:, 0:KB, 1:9], A_)
                e.drain()
                e.tensor_copy(hh[:, :, T:TOK], hs)
                e.drain()
                tt(hl[:, :, T:TOK], hs, hh[:, :, T:TOK].bitcast(F32), S_).then_inc(hs_ready, 1)
                for kb in range(KB + 1):
                    if kb < KB:
                        stt((t1, t2)[kb % 2][:, 0:T], o[:, kb, 0:T], ag[:, kb, 0:1], t3[:, 0:T], M, M).then_inc(hn_ready, 1)
                    if kb:
                        e.wait_ge(h_hi, l * KB + kb)
                        stt(hl[:, kb - 1, 0:T], (t1, t2)[(kb - 1) % 2][:, 0:T], mod[:, kb - 1, 0:1],
                            hh[:, kb - 1, 0:T].bitcast(F32), A_, S_).then_inc(h_ready, 1)
                    e.drain()
                e.wait_ge(y_saved, (l + 1) * 16)

                for count, base, kind, _cols in GROUPS:
                    if kind == "ml":
                        G = slice(0, H_ML)
                        e.wait_ge(gsem["a1"], l + 1)
                        ig, fg = t1[G, :], t2[G, :]
                        b6, m_, u6 = lev[G, 0, :], lev[G, 1, :], lev[G, 2, :]
                        stt(fg, fg, 0.0, t3[G, :], MIN, S_)
                        e.drain()
                        chunk_sums(b6, fg, G)
                        e.tensor_tensor_scan(m_, fg[:, 0:T], ig[:, 0:T], 0.0, A_, MAX)
                        tt(g8[:, 6, :], fg[:, T:TOK], m6[:], A_)
                        e.drain()
                        tt(g8[:, 3, :], g8[:, 6, :], ig[:, T:TOK], MAX)
                        tt(r6, b6, m_, S_)
                        tt(u6, ig[:, 0:T], b6, S_)
                        e.tensor_copy(g4[:, 0, 1:NC], m_[:, CH - 1:T - 1:CH])
                        e.tensor_copy(g4[:, 3, :], m_[:, CH - 1:T:CH])
                        e.drain()
                        tt(g8[:, 4, :], g8[:, 6, :], g8[:, 3, :], S_)
                        tt(g8[:, 5, :], ig[:, T:TOK], g8[:, 3, :], S_)
                        e.tensor_copy(g4[:, 1, :], r6[:, CH - 1:T:CH])
                        e.drain()
                        tt(g4[:, 2, :], g4[:, 1, :], g4[:, 0, :], A_)
                        tt(iw6[:].rearrange("p (c t) -> p c t", c=NC), r6.rearrange("p (c t) -> p c t", c=NC),
                           bc(g4[:, 0, :], 2, CH), A_)
                        tt(lev[G, 3, :].rearrange("p (c t) -> p c t", c=NC), u6.rearrange("p (c t) -> p c t", c=NC),
                           bc(g4[:, 1, :], 2, CH), A_)
                        e.tensor_copy(lev[G, 4, :], m_)
                        e.drain().then_inc(gsem["v1"], 1)
                        e.wait_ge(gsem["a2"], l + 1)
                        tt(lev[G, 5, 0:H_ML * NC].rearrange("p (h c) -> p h c", c=NC), bc(g4[:, 2, :], 1, H_ML),
                           bc(cst[G, C_ID:C_ID + H_ML], 2, NC), M)
                        tt(lev[G, 5, 64:64 + H_ML * NS].rearrange("p (h c) -> p h c", c=NS), bc(g8[:, 0, :], 1, H_ML),
                           bc(cst[G, C_ID:C_ID + H_ML], 2, NS), M)
                        e.drain().then_inc(gsem["v2"], 1)
                        e.wait_ge(gsem["tr"], l + 1)
                        e.tensor_copy(gcol[:, :, 0:3, :].rearrange("p h w c -> p w c h"),
                                      mx[:, 1, 0:96].rearrange("p (w c x) -> p w c x", w=3, x=8)[:, :, :, 0:H_ML])
                        e.tensor_copy(gcol[:, :, 3, :], mx[:, 3, 0:H_ML * NC].rearrange("p (h c) -> p h c", c=NC))
                        e.tensor_copy(gs[:].rearrange("p h w -> p w h"),
                                      mx[0:NS, 2, 0:24].rearrange("p (w x) -> p w x", x=8)[:, :, 0:H_ML])
                        e.tensor_copy(gsb[:], mx[:, 3, 64:64 + H_ML * NS].rearrange("p (h s) -> p h s", s=NS))
                        e.drain().then_inc(gsem["col"], 1)

                    with e.Fori(0, count) as i:
                        g = i + (l * NH + base)
                        n = i + l * count

                        def gain():
                            e.tensor_copy(sm[:, 32:33], prm[:, bass.ds(i + (R_GN + base), 1)])

                        def blocks(src, dst):
                            tt(dst.rearrange("p (s d) -> p s d", s=NS), bc(src, 1, NS),
                               bc(cst[0:NS, C_ID:C_ID + NS], 2, HD), M)

                        def rope(j, dst):
                            e.wait_ge(ps[("rot_q", "rot_k")[j]], n + 1)
                            tt(dst[:], (x0, x1)[j][:, PAD:PAD + TOK], rope_t[:, 0:TOK], M)
                            for b in range(2):
                                tt(t1[:, b * HALF:(b + 1) * HALF], mx[:, 2 * j + b, 0:HALF],
                                   rope_t[:, TOK + b * HALF:TOK + (b + 1) * HALF], M)
                            e.drain()
                            tt(dst[:], dst[:], t1[:], A_)
                            e.drain()

                        def conv(j, dst, name):
                            src = (x0, x1)[j]
                            w = [sm[:, 48 + 2 * m + j:49 + 2 * m + j] for m in range(CONV_W)]
                            cb = sm[:, 56 + j:57 + j]
                            old = cvc[:, j, :].rearrange("p (s r) -> p s r", r=PAD)
                            ts(dst[:, 0:T], src[:, 0:T], w[0], cb, M, A_)
                            ts(dst[:, T:TOK], old[:, :, 0], w[0], cb, M, A_)
                            for m in range(1, CONV_W):
                                e.drain()
                                stt(dst[:, 0:T], src[:, m:m + T], w[m], dst[:, 0:T], M, A_)
                                x = old[:, :, m] if m < PAD else src[:, PAD + T:PAD + TOK]
                                stt(dst[:, T:TOK], x, w[m], dst[:, T:TOK], M, A_)
                            e.drain().then_inc(vs[name], 1)

                        if kind == "rt":
                            gain()
                            e.wait_ge(aux_in, auxc(l, kind, i))
                            rope(0, q)
                            tt(qd[:], q[:, 0:T], hc[:, HC_IN:HC_IN + T], M)
                            e.tensor_copy(sm[:, 16:20], hc[:, HC_CD:HC_CD + NC])
                            e.tensor_copy(sm[:, 24:32], hc[:, HC_G:HC_G + NS])
                            rope(1, k)
                            e.drain().then_inc(vs["qk"], 1)
                            e.wait_ge(ps["score"], scorec(l, kind, i, 1))
                            tt(a, mx[:, 0, :].rearrange("p (c t) -> p c t", c=NC), bc(hc[:, HC_D:HC_D + CH], 1, NC),
                               M)
                            e.drain().then_inc(vs["a"], 1)
                        elif kind == "ml":
                            gain()
                            e.tensor_copy(sm[:, 33:34], prm[:, bass.ds(i + R_SKIP, 1)])
                            for m in range(2 * CONV_W):
                                e.tensor_copy(sm[:, 48 + m:49 + m], prm[:, bass.ds(i + (R_CW + m * H_ML), 1)])
                            for j in range(2):
                                e.tensor_copy(sm[:, 56 + j:57 + j], prm[:, bass.ds(i + (R_CB + j * H_ML), 1)])
                            gh = gcol[:, bass.ds(i, 1)].rearrange("p h w c -> p (h w) c")
                            e.tensor_copy(sm[:, 0:8].rearrange("p (w c) -> p w c", w=2), gh[:, 0:2, :])
                            e.tensor_copy(sm[:, 12:20].rearrange("p (w c) -> p w c", w=2), gh[:, 2:4, :])
                            e.tensor_copy(sm[:, 24:32], gsb[:, bass.ds(i, 1)].rearrange("p h s -> p (h s)"))
                            e.tensor_copy(sm[0:NS, 60:63], gs[:, bass.ds(i, 1)].rearrange("p h w -> p (h w)"))
                            e.drain()
                            e.wait_ge(ps["bcast"], n + 1)
                            tt(dt[:].rearrange("p (c t) -> p c t", c=NC), mx[:, 0, :].rearrange("p (c t) -> p c t", c=NC),
                               bc(sm[:, 0:4], 2, CH), A_)
                            e.tensor_copy(lev[:, 2, :], mx[:, 1, :])
                            e.drain()
                            tt(dt[:].rearrange("p (c t) -> p c t", c=NC), dt[:].rearrange("p (c t) -> p c t", c=NC),
                               bc(cst[:, C_NEG:C_NEG + 128], 1, NC), A_)
                            e.drain().then_inc(vs["r"], 1)
                            e.wait_ge(taken, ht(g, 0))
                            e.wait_ge(as_["cvc"], n + 1)
                            conv(0, t1, "conv_q")
                            e.wait_ge(as_["silu"], 2 * n + 1)
                            ts(t3[:], t3[:], 1.0, None, A_)
                            e.drain()
                            e.reciprocal(t3[:], t3[:])
                            e.drain()
                            tt(q[:], t1[:], t3[:], M)
                            e.wait_ge(taken, ht(g, 1))
                            conv(1, t2, "conv_k")
                            e.wait_ge(as_["silu"], 2 * n + 2)
                            ts(t4[:], t4[:], 1.0, None, A_)
                            tt(qd[:], q[:, 0:T], lev[:, 2, :], M)
                            e.drain()
                            e.reciprocal(t4[:], t4[:])
                            e.drain().then_inc(vs["qd"], 1)
                            e.drain()
                            stt(k[:], t2[:], SCALE, t4[:], M, M)
                            e.drain().then_inc(vs["qk"], 1)
                            e.wait_ge(ps["score"], scorec(l, kind, i, 1))
                            tt(t1[:, 0:T], mx[:, 0, :], dt[:], M)
                            e.drain().then_inc(vs["a"], 1)
                        else:
                            gain()
                            e.tensor_copy(sm[:, 8:9], lbc[:, 0, bass.ds(i, 1)])
                            e.tensor_copy(sm[:, 9:10], lbc[:, 1, bass.ds(i, 1)])
                            e.drain()
                            e.wait_ge(as_["l1"], n + 1)
                            f = x0[:, PAD:PAD + TOK]
                            stt(t2[:], f, 0.0, t1[:], MIN, S_)
                            e.drain()
                            tt(t4[:], t2[:], f, S_)
                            ts(t3[:], t2[:], sm[:, 9:10], sm[:, 8:9], A_, S_)
                            e.drain()
                            absolute(t3[:], t3[:])
                            ts(t2[:], t2[:], sm[:, 9:10], sm[:, 8:9], A_, MAX)
                            e.drain().then_inc(vs["d1"], 1)
                            e.wait_ge(as_["l2"], n + 1)
                            tt(t3[:], t2[:], t3[:], A_)
                            e.drain()
                            chunk_sums(t2, t3, slice(0, P))
                            e.drain()
                            bb = t2[:, 0:T].rearrange("p (c t) -> p c t", c=NC)
                            tt(t4[:, 0:T].rearrange("p (c t) -> p c t", c=NC), bb,
                               bc(t2[:, CH - 1:T:CH], 2, CH), S_)
                            e.drain().then_inc(vs["b"], 1)
                            for lv in range(LEVELS):
                                x = 64 >> lv
                                nb = T // (2 * x)
                                src = t2[:, 0:T].rearrange("p (n y) -> p n y", y=2 * x)
                                tt(lev[:, lv, :].rearrange("p (n y) -> p n y", y=2 * x), src,
                                   src[:, :, x - 1:x].broadcast_to([P, nb, 2 * x]), S_).then_inc(vs["lf"], 1)
                            e.wait_ge(taken, ht(g, 1))
                            e.wait_ge(as_["eb"], n + 1)
                            e.wait_ge(as_["kk"], n + 1)
                            e.sem_inc(vs["qk"], 1)
                            qq = x1[:, PAD:PAD + T]
                            tt(qd[:], qd[:], qq, M)
                            tt(dt[:], dt[:], k[:, 0:T], M)
                            e.drain().then_inc(vs["kw"], 1)
                            for lv in range(LEVELS):
                                e.wait_ge(as_["lev"], n * LEVELS + (lv + 1))
                                x = 64 >> lv
                                w = lev[:, lv, :].rearrange("p (n s x) -> p n s x", s=2, x=x)
                                kv = k[:, 0:T].rearrange("p (n s x) -> p n s x", s=2, x=x)
                                qv = qq.rearrange("p (n s x) -> p n s x", s=2, x=x)
                                tt(w[:, :, 0, :], w[:, :, 0, :], kv[:, :, 0, :], M)
                                tt(w[:, :, 1, :], w[:, :, 1, :], qv[:, :, 1, :], M)
                                e.drain().then_inc(vs["lev"], 1)
                            for lv in range(-1, LEVELS):
                                e.wait_ge(ps["score"], scorec(l, kind, i, lv + 2))
                                bank = mx[:, (lv + 1) % 4, :].rearrange("p (c t) -> p c t", c=NC)
                                if lv < 0:
                                    tt(a, bank, bc(ident, 1, NC), M)
                                else:
                                    held(e)
                                    mk = lmask[:, 128 * lv:128 * lv + 128]
                                    e.copy_predicated(a, bc(mk, 1, NC), bank)
                                e.drain().then_inc(vs["pred"], 1)
                            e.drain().then_inc(vs["a"], 1)

                        e.wait_ge(as_["sr"], g + 1)
                        if kind == "ml":
                            ts(sw[:], sr[:, 1, :], sm[0:NS, 61:62], None, M)
                            e.drain()
                            e.wait_ge(aux_in, auxc(l, kind, i))
                            stt(nr[:], nr[:], sm[0:NS, 60:61], sw[:], M, A_)
                            e.drain().then_inc(vs["nrow"], 1)
                            e.tensor_tensor_reduce(out=t3[0:NS, 0:HD], in0=nr[:], in1=sr[:, 0, :], scale=1.0, scalar=0.0,
                                                   op0=M, op1=A_, accum_out=sm[0:NS, 63:64])
                            ts(sw[:], sr[:, 2, :], sm[0:NS, 61:62], None, M)
                            e.memset(vt[:, :, HD:HD + 1], 1.0)
                            blocks(sr[:, 1, :], big[0:NS, :])
                            blocks(sr[:, 0, :], lev[0:NS, 0:2, :].rearrange("p a b -> p (a b)"))
                        else:
                            blocks(sr[:, 2, :], big[0:NS, :])
                        e.drain().then_inc(vs["blk"], 1)
                        e.wait_ge(state_in, (g + 1) * 16)
                        e.wait_ge(ps["u"], g + 1)
                        w = HD + 1 if kind == "ml" else HD
                        for c in range(NC):
                            uc = mx[:, c // 2, (c % 2) * 129:(c % 2) * 129 + w]
                            if c == 0:
                                e.tensor_copy(st[:, 0, 0:w], uc)
                            else:
                                stt(st[:, c, 0:w], st[:, c - 1, 0:w], sm[:, 16 + c:17 + c], uc, M, A_)
                            e.drain()
                        e.drain().then_inc(vs["chain"], 1)
                        tt(ss[:], ss[:], bc(sm[:, 24:32], 2, HD), M)
                        e.drain()
                        e.wait_ge(ps["outer"], g + 1)
                        tt(ss[:].rearrange("p s v -> p (s v)"), ss[:].rearrange("p s v -> p (s v)"),
                           mx[:, 2:4, :].rearrange("p b n -> p (b n)"), A_)
                        e.drain().then_inc(vs["ss"], 1)

                        e.wait_ge(ps["o"], g + 1)
                        ov = mx[:, 0:2, 0:258].rearrange("p b (c d) -> p b c d", c=2)
                        hv = ho.rearrange("p (b c) d -> p b c d", b=2)
                        if kind == "ml":
                            den = sm[:, 34:38]
                            den4 = den.rearrange("p (b c) -> p b c", b=2)
                            e.tensor_copy(den4, ov[:, :, :, HD])
                            e.drain()
                            absolute(den, den)
                            e.drain()
                            tt(den, den, sm[:, 12:16], MAX)
                            e.drain()
                            e.reciprocal(den, den)
                            e.drain()
                            tt(hv, ov[:, :, :, 0:HD], den4.unsqueeze(3).broadcast_to([P, 2, 2, HD]), M)
                        else:
                            e.tensor_copy(hv, ov[:, :, :, 0:HD])
                        e.drain()
                        e.wait_ge(ps["os"], g + 1)
                        if kind == "ml":
                            qb = mx[:, 2:4, :].rearrange("p b n -> p (b n)")
                            tt(big, ss[:].rearrange("p s v -> p (s v)"), qb, M)
                            e.drain()
                            e.reduce_sum(sm[:, 40:48], big.rearrange("p (s d) -> p s d", s=NS), axis=mybir.AxisListType.X)
                            absolute(sm[0:NS, 63:64], sm[0:NS, 63:64])
                            e.drain().then_inc(vs["osc"], 1)
                            tt(sm[0:NS, 63:64], sm[0:NS, 63:64], sm[0:NS, 62:63], MAX)
                            e.drain()
                            e.reciprocal(sm[0:NS, 63:64], sm[0:NS, 63:64])
                            e.drain()
                            e.wait_ge(ps["ostr"], n + 1)
                            ts(hos[:], mx[0:NS, 2, 0:HD], sm[0:NS, 63:64], None, M)
                        else:
                            tt(big[0:NS, :].rearrange("p (s d) -> p s d", s=NS),
                               mx[0:NS, 2:4, :].rearrange("p b (s d) -> p (b s) d", d=HD),
                               bc(cst[0:NS, C_ID:C_ID + NS], 2, HD), M)
                            e.drain()
                            e.reduce_sum(hos[:], big[0:NS, :].rearrange("p (s d) -> p d s", s=NS),
                                         axis=mybir.AxisListType.X)
                        e.drain()
                        for c in range(NC + 1):
                            r = slice(0, P if c < NC else NS)
                            e.bn_stats(bst[r, c, :], ho[:, c, :] if c < NC else hos[:])
                        e.drain()
                        for c in range(NC + 1):
                            r = slice(0, P if c < NC else NS)
                            e.bn_aggr(bag[r, c, :], bst[r, c, :])
                        e.drain()
                        for r, cs in ((slice(0, P), slice(0, NC)), (slice(0, NS), slice(NC, NC + 1))):
                            mean, var = bag[r, cs, 0], bag[r, cs, 1]
                            if kind == "hg":
                                tt(mean, mean, mean, M)
                                e.drain()
                                tt(var, var, mean, A_)
                                e.drain()
                            ts(var, var, EPS, None, A_)
                        e.drain().then_inc(vs["var"], 1)
                        e.wait_ge(as_["rs"], g + 1)
                        for c in range(NC + 1):
                            r = slice(0, P if c < NC else NS)
                            hc_ = ho[:, c, :] if c < NC else hos[:]
                            if kind == "hg":
                                ts(hc_, hc_, rstd[r, c:c + 1], None, M)
                            else:
                                ts(hc_, hc_, bag[r, c, 0:1], rstd[r, c:c + 1], S_, M)
                        e.drain().then_inc(vs["ho"], 1)
                        e.wait_ge(as_["z"], g + 1)
                        ts(t4[:], t4[:], 1.0, None, A_)
                        e.drain()
                        e.reciprocal(t4[:], t4[:])
                        e.drain()
                        tt(z, z, t4[:], M)
                        e.drain()
                        e.wait_ge(ps["back"], g + 1)
                        dst = o[:, bass.ds(i + base, 1), :].rearrange("p h t -> p (h t)")
                        if kind == "ml":
                            e.wait_ge(as_["ct"], n + 1)
                            ts(t2[:], q[:], sm[:, 33:34], None, M)
                            e.drain()
                            stt(t2[:, 0:T], mx[:, 2, :], sm[:, 32:33], t2[:, 0:T], M, A_)
                            stt(t2[:, T:TOK], mx[:, 3, 0:NS], sm[:, 32:33], t2[:, T:TOK], M, A_)
                            e.drain()
                            tt(dst, t2[:], z, M)
                        else:
                            stt(dst[:, 0:T], mx[:, 2, :], sm[:, 32:33], z[:, 0:T], M, M)
                            stt(dst[:, T:TOK], mx[:, 3, 0:NS], sm[:, 32:33], z[:, T:TOK], M, M)
                        e.drain().then_inc(head_done, 1)

                for n in range(KB):
                    e.wait_ge(y_in[n % 4], (l * (KB // 4) + n // 4 + 1) * 16)
                    e.wait_ge(tile_done, l * TILES + 4 * NH + n + 1)
                    gt, yt = mod[:, 2 * KB + n, :], y_tile(n)
                    p0, p1 = pj[:, 2 * (n % 2), 0:HALF], pj[:, 2 * (n % 2) + 1, 0:HALF]
                    stt(o[:, n, 0:HALF], p0, gt[:, 0:1], yt[:, 0:HALF], M, A_)
                    stt(o[:, n, HALF:T], p1[:, 0:T - HALF], gt[:, 0:1], yt[:, HALF:T], M, A_)
                    tt(sm[:, 0:NS], p1[:, T - HALF:HALF], gt[:, 1:9], M)
                    e.drain()
                    tt(o[:, n, T:TOK], yt[:, T:TOK], sm[:, 0:NS], A_)
                    e.drain().then_inc(out_added, 1)
            norm(DEPTH)
            e.drain().then_inc(rs_ready, 1)
            for kb in range(KB):
                stt(o[:, kb, :], o[:, kb, :], bia[:, 3 * KB + kb:3 * KB + kb + 1], t3[:], M, M).then_inc(fin_n, 1)


_IN = ["x_prompt", "x_sample", "state_hgrn", "state_mlstm_C", "state_mlstm_n", "state_mlstm_m", "state_mlstm_conv",
       "state_ret", "c_prompt", "c_sample", "g_norm", "w_ada", "b_ada", "w_in", "hgrn_lb", "mlstm_conv_w",
       "mlstm_conv_b", "mlstm_b_i", "mlstm_b_f", "mlstm_skip", "w_gn", "w_out", "g_final"]


def _states(b):
    return [(DEPTH, b, H_HG, HD, HD), (DEPTH, b, H_ML, HD, HD), (DEPTH, b, H_ML, HD), (DEPTH, b, H_ML),
            (DEPTH, b, PAD, 2 * W_ML), (DEPTH, b, H_RT, HD, HD)]


_OUT = [(1, T, D), (NS, 1, D)] + _states(1) + _states(NS)


def kernel(**inputs):
    import concourse.bacc as bacc
    from concourse.bass_utils import run_bass_kernel_spmd as run

    nc = bacc.Bacc("TRN2", target_bir_lowering=False, num_devices=1)
    arrays, args = {}, []
    given = [(n, np.ascontiguousarray(inputs[n])) for n in _IN] + list(zip(("cst", "hc", "rope", "sel", "lm"), constants()))
    for name, arr in given:
        arrays["in_" + name] = arr
        args.append(nc.dram_tensor("in_" + name, arr.shape, mybir.dt.from_np(arr.dtype), kind="ExternalInput").ap())
    for i, shape in enumerate(_OUT):
        args.append(nc.dram_tensor(f"out_{i}", shape, F32, kind="ExternalOutput").ap())
    program(nc, *args)
    r = run(nc, [arrays], core_ids=[0])
    return tuple(r.results[0][f"out_{i}"] for i in range(len(_OUT)))
```
